# Optimizing a Trainium2 kernel written in Bass

```python
import math
import jax
import jax.numpy as jnp
from jax import lax
import numpy as np
import jax, jax.numpy as jnp

D_MODEL = 1024
BATCH = 1
SEQ = 256
DEPTH = 2

N_MIXERS = 2
N_MLA_LAYERS = (DEPTH + 1) // 2
N_DIL_LAYERS = DEPTH // 2

MLA_HEADS = 16
MLA_NOPE = 64
MLA_ROPE = 32
MLA_QK = MLA_NOPE + MLA_ROPE
MLA_V = 64
Q_LORA = 3 * D_MODEL // 8
KV_LORA = D_MODEL // 4
MLA_IN = Q_LORA + KV_LORA + MLA_ROPE
ROPE_THETA = 10000.0
Q_BLOCK = 128

DIL_GROUPS = ((128, 1), (512, 4), (2048, 16))
N_DIL_GROUPS = len(DIL_GROUPS)
DIL_HEADS = 16
DIL_HEAD_DIM = 64
DIL_IN = N_DIL_GROUPS * 3 * DIL_HEADS * DIL_HEAD_DIM

N_BUCKETS = 32
MAX_DISTANCE = 1024

D_FF = 4 * D_MODEL
N_MOD = 6
EPS = 1e-6


def rms_norm(x, g):
    xf = x.astype(jnp.float32)
    y = xf * lax.rsqrt(jnp.mean(xf * xf, axis=-1, keepdims=True) + EPS)
    return (y * g.astype(jnp.float32)).astype(x.dtype)

def rope(x, pos):
    half = x.shape[-1] // 2
    inv = 1.0 / (ROPE_THETA ** (jnp.arange(half, dtype=jnp.float32) / half))
    ang = pos.astype(jnp.float32)[..., None] * inv
    ang = ang.reshape(ang.shape[:2] + (1,) * (x.ndim - 3) + (half,))
    cos, sin = jnp.cos(ang), jnp.sin(ang)
    x1 = x[..., :half].astype(jnp.float32)
    x2 = x[..., half:].astype(jnp.float32)
    out = jnp.concatenate([x1 * cos - x2 * sin, x2 * cos + x1 * sin], axis=-1)
    return out.astype(x.dtype)

def t5_bucket(rel):
    nb = N_BUCKETS // 2
    max_exact = nb // 2
    ret = jnp.where(rel > 0, nb, 0)
    n = jnp.abs(rel)
    nf = jnp.maximum(n, 1).astype(jnp.float32)
    large = max_exact + (jnp.log(nf / max_exact) / math.log(MAX_DISTANCE / max_exact)
                         * (nb - max_exact)).astype(jnp.int32)
    large = jnp.minimum(large, nb - 1)
    return ret + jnp.where(n < max_exact, n, large)

def dense_attention(q, k, v, scale):
    B, S, H, Dk = q.shape
    nq = S // Q_BLOCK
    qb = jnp.moveaxis(q.reshape(B, nq, Q_BLOCK, H, Dk), 1, 0)

    def block(qi):
        s = jnp.einsum('bqhd,bkhd->bhqk', qi, k, preferred_element_type=jnp.float32) * scale
        p = jax.nn.softmax(s, axis=-1).astype(v.dtype)
        return jnp.einsum('bhqk,bkhd->bqhd', p, v)

    o = lax.map(block, qb)
    return jnp.moveaxis(o, 0, 1).reshape(B, S, H, v.shape[-1])

def mla_mixer(h, pos, w_in, g_qa, w_qb, g_kva, w_kvb, g_q, g_k, w_o):
    B, S, _ = h.shape
    proj = h @ w_in
    q_lat = proj[..., :Q_LORA]
    kv_lat = proj[..., Q_LORA:Q_LORA + KV_LORA]
    k_rope = rope(proj[..., Q_LORA + KV_LORA:], pos)
    q = (rms_norm(q_lat, g_qa) @ w_qb).reshape(B, S, MLA_HEADS, MLA_QK)
    kv = (rms_norm(kv_lat, g_kva) @ w_kvb).reshape(B, S, MLA_HEADS, MLA_NOPE + MLA_V)
    q = jnp.concatenate([q[..., :MLA_NOPE], rope(q[..., MLA_NOPE:], pos)], axis=-1)
    k = jnp.concatenate([kv[..., :MLA_NOPE],
                         jnp.broadcast_to(k_rope[:, :, None, :], (B, S, MLA_HEADS, MLA_ROPE))],
                        axis=-1)
    v = kv[..., MLA_NOPE:]
    q = rms_norm(q, g_q)
    k = rms_norm(k, g_k)
    o = dense_attention(q, k, v, MLA_QK ** -0.5)
    return o.reshape(B, S, MLA_HEADS * MLA_V) @ w_o

def _to_residues(t, dilation):
    B, S = t.shape[:2]
    L = S // dilation
    t = t.reshape((B, L, dilation) + t.shape[2:])
    t = jnp.moveaxis(t, 2, 1)
    return t.reshape((B * dilation, L) + t.shape[3:])

def _from_residues(t, batch, dilation):
    L = t.shape[1]
    t = t.reshape((batch, dilation, L) + t.shape[2:])
    t = jnp.moveaxis(t, 1, 2)
    return t.reshape((batch, L * dilation) + t.shape[3:])

def dilated_group(q, k, v, pos, bias_table, window, dilation):
    B, S, H, Dh = q.shape
    half = window // (2 * dilation)
    blk = half
    L = S // dilation
    nb = -(-L // blk)
    Lp = nb * blk
    padq = Lp - L
    N = B * dilation
    qr, kr, vr, pr = (_to_residues(t, dilation) for t in (q, k, v, pos))
    qb = jnp.pad(qr, ((0, 0), (0, padq), (0, 0), (0, 0))).reshape(N, nb, blk, H, Dh)

    def key_blocks(t):
        pad = [(0, 0), (blk, padq + blk)] + [(0, 0)] * (t.ndim - 2)
        t = jnp.pad(t, pad).reshape((N, nb + 2, blk) + t.shape[2:])
        return jnp.concatenate([t[:, :-2], t[:, 1:-1], t[:, 2:]], axis=2)

    kb, vb, pk = key_blocks(kr), key_blocks(vr), key_blocks(pr)
    pq = jnp.pad(pr, ((0, 0), (0, padq))).reshape(N, nb, blk)
    qi = jnp.arange(nb)[:, None] * blk + jnp.arange(blk)[None, :]
    ki = jnp.arange(nb)[:, None] * blk - blk + jnp.arange(3 * blk)[None, :]
    valid = ((ki[:, None, :] >= 0) & (ki[:, None, :] < L)
             & (jnp.abs(qi[:, :, None] - ki[:, None, :]) <= half))
    bucket = t5_bucket(pk[:, :, None, :] - pq[:, :, :, None])
    bias = jnp.moveaxis(bias_table[bucket], -1, 2).astype(jnp.float32)
    s = jnp.einsum('nbqhd,nbkhd->nbhqk', qb, kb,
                   preferred_element_type=jnp.float32) * (DIL_HEAD_DIM ** -0.5) + bias
    s = jnp.where(valid[None, :, None], s, -jnp.inf)
    lse = jax.nn.logsumexp(s, axis=-1)
    p = jnp.exp(s - lse[..., None]).astype(v.dtype)
    o = jnp.einsum('nbhqk,nbkhd->nbqhd', p, vb).reshape(N, Lp, H, Dh)[:, :L]
    lse = jnp.moveaxis(lse, 2, 3).reshape(N, Lp, H)[:, :L]
    return _from_residues(o, B, dilation), _from_residues(lse, B, dilation)

def dilated_mixer(h, pos, w_in, g_q, g_k, rel_bias, w_o):
    B, S, _ = h.shape
    proj = (h @ w_in).reshape(B, S, N_DIL_GROUPS, 3, DIL_HEADS, DIL_HEAD_DIM)
    outs, lses = [], []
    for gi, (window, dilation) in enumerate(DIL_GROUPS):
        q = rms_norm(proj[:, :, gi, 0], g_q[gi])
        k = rms_norm(proj[:, :, gi, 1], g_k[gi])
        v = proj[:, :, gi, 2]
        table = rel_bias[:, gi * DIL_HEADS:(gi + 1) * DIL_HEADS]
        o, lse = dilated_group(q, k, v, pos, table, window, dilation)
        outs.append(o)
        lses.append(lse)
    o_all = jnp.stack(outs, axis=0)
    wts = jax.nn.softmax(jnp.stack(lses, axis=0), axis=0)
    o = jnp.einsum('gbsh,gbshd->bshd', wts.astype(o_all.dtype), o_all)
    return o.reshape(B, S, DIL_HEADS * DIL_HEAD_DIM) @ w_o

def first_inputs(seed: int = 0) -> dict:
    key = jax.random.key(seed)
    ks = jax.random.split(key, 24)
    f32 = jnp.float32
    nrm = lambda k, shape, s: jax.random.normal(k, shape, f32) * s
    gain = lambda k, shape: 1.0 + 0.05 * jax.random.normal(k, shape, f32)
    D = D_MODEL
    return {
        "x": nrm(ks[0], (BATCH, SEQ, D), 1.0),
        "c": nrm(ks[1], (BATCH, D), 1.0),
        "positions": jnp.broadcast_to(jnp.arange(SEQ, dtype=jnp.int32), (BATCH, SEQ)),
        "ada_w": nrm(ks[2], (DEPTH, D, N_MOD * D), 0.5 * D ** -0.5),
        "ada_b": nrm(ks[3], (DEPTH, N_MOD * D), 0.02),
        "norm_mix": gain(ks[4], (DEPTH, D)),
        "norm_mlp": gain(ks[5], (DEPTH, D)),
        "mlp_w1": nrm(ks[6], (DEPTH, D, D_FF), D ** -0.5),
        "mlp_w2": nrm(ks[7], (DEPTH, D_FF, D), D_FF ** -0.5),
        "mla_w_in": nrm(ks[8], (N_MLA_LAYERS, D, MLA_IN), D ** -0.5),
        "mla_g_qa": gain(ks[9], (N_MLA_LAYERS, Q_LORA)),
        "mla_w_qb": nrm(ks[10], (N_MLA_LAYERS, Q_LORA, MLA_HEADS * MLA_QK), Q_LORA ** -0.5),
        "mla_g_kva": gain(ks[11], (N_MLA_LAYERS, KV_LORA)),
        "mla_w_kvb": nrm(ks[12], (N_MLA_LAYERS, KV_LORA, MLA_HEADS * (MLA_NOPE + MLA_V)), KV_LORA ** -0.5),
        "mla_g_q": gain(ks[13], (N_MLA_LAYERS, MLA_QK)),
        "mla_g_k": gain(ks[14], (N_MLA_LAYERS, MLA_QK)),
        "mla_w_o": nrm(ks[15], (N_MLA_LAYERS, MLA_HEADS * MLA_V, D), (MLA_HEADS * MLA_V) ** -0.5),
        "dil_w_in": nrm(ks[16], (N_DIL_LAYERS, D, DIL_IN), D ** -0.5),
        "dil_g_q": gain(ks[17], (N_DIL_LAYERS, N_DIL_GROUPS, DIL_HEAD_DIM)),
        "dil_g_k": gain(ks[18], (N_DIL_LAYERS, N_DIL_GROUPS, DIL_HEAD_DIM)),
        "dil_w_o": nrm(ks[19], (N_DIL_LAYERS, DIL_HEADS * DIL_HEAD_DIM, D), (DIL_HEADS * DIL_HEAD_DIM) ** -0.5),
        "rel_bias": nrm(ks[20], (N_BUCKETS, N_DIL_GROUPS * DIL_HEADS), 0.3),
    }

def first_block(x, c, positions, ada_w, ada_b, norm_mix, norm_mlp, mlp_w1, mlp_w2,
              mla_w_in, mla_g_qa, mla_w_qb, mla_g_kva, mla_w_kvb, mla_g_q, mla_g_k, mla_w_o,
              dil_w_in, dil_g_q, dil_g_k, dil_w_o, rel_bias):
    B, S, D = x.shape
    cond = jax.nn.silu(c)
    for i in range(DEPTH):
        mod = (cond @ ada_w[i] + ada_b[i]).reshape(B, N_MOD, D)
        shift1, scale1, gate1 = mod[:, 0, None, :], mod[:, 1, None, :], mod[:, 2, None, :]
        shift2, scale2, gate2 = mod[:, 3, None, :], mod[:, 4, None, :], mod[:, 5, None, :]
        h = rms_norm(x, norm_mix[i]) * (1 + scale1) + shift1
        j = i // N_MIXERS
        if i % N_MIXERS == 0:
            y = mla_mixer(h, positions, mla_w_in[j], mla_g_qa[j], mla_w_qb[j], mla_g_kva[j],
                          mla_w_kvb[j], mla_g_q[j], mla_g_k[j], mla_w_o[j])
        else:
            y = dilated_mixer(h, positions, dil_w_in[j], dil_g_q[j], dil_g_k[j], rel_bias, dil_w_o[j])
        x = x + gate1 * y
        h = rms_norm(x, norm_mlp[i]) * (1 + scale2) + shift2
        x = x + gate2 * (jnp.square(jax.nn.relu(h @ mlp_w1[i])) @ mlp_w2[i])
    return x


DEPTH_2 = 1

CHUNK = 64
MIX_WIDTH = D_MODEL
LRU_WIDTH = MIX_WIDTH // 2
LRU_BLOCKS = 8
LRU_BLOCK = LRU_WIDTH // LRU_BLOCKS
CONV_WIDTH = 4
LRU_C = 8.0
ATT_WIDTH = MIX_WIDTH - LRU_WIDTH
ATT_HEADS = 8
ATT_HEAD_DIM = ATT_WIDTH // ATT_HEADS
LEFT_CHUNKS = 8
BAND_CHUNKS = LEFT_CHUNKS + 1
REL_CLIP = 128
MEM_LEN = 256
MEM_HEADS = 4
MEM_HEAD_DIM = D_MODEL // MEM_HEADS
PEER_HEADS = 8
N_KEYS = 128
N_EXPERTS = N_KEYS * N_KEYS
PEER_TOPK = 16
PEER_KEY_DIM = 128
PEER_QUERY_DIM = 2 * PEER_KEY_DIM
PEER_BLOCK = 128
IN_WIDTH = 2 * LRU_WIDTH + 3 * ATT_WIDTH
NEG_INF = -1e30


def _rmsnorm(x, g):
    xf = x.astype(jnp.float32)
    y = xf * lax.rsqrt(jnp.mean(xf * xf, axis=-1, keepdims=True) + EPS)
    return (y * g.astype(jnp.float32)).astype(x.dtype)

def _rg_lru(xr, conv_w, conv_b, gate_a_w, gate_a_b, gate_x_w, gate_x_b, lru_lambda):
    B, S, _ = xr.shape
    xc = lax.conv_general_dilated(
        xr, conv_w[:, None, :], window_strides=(1,), padding=[(CONV_WIDTH - 1, 0)],
        dimension_numbers=('NWC', 'WIO', 'NWC'), feature_group_count=LRU_WIDTH) + conv_b
    xb = xc.reshape(B, S, LRU_BLOCKS, LRU_BLOCK)
    r = jax.nn.sigmoid((jnp.einsum('bshi,hij->bshj', xb, gate_a_w).reshape(B, S, LRU_WIDTH)
                        + gate_a_b).astype(jnp.float32))
    i = jax.nn.sigmoid((jnp.einsum('bshi,hij->bshj', xb, gate_x_w).reshape(B, S, LRU_WIDTH)
                        + gate_x_b).astype(jnp.float32))
    log_a = -LRU_C * r * jax.nn.softplus(-lru_lambda.astype(jnp.float32))
    a = jnp.exp(log_a)
    mult = jnp.sqrt(jnp.maximum(-jnp.expm1(2.0 * log_a), 0.0))
    b = mult * i * xc.astype(jnp.float32)

    def combine(left, right):
        a1, b1 = left
        a2, b2 = right
        return a1 * a2, a2 * b1 + b2

    _, h = lax.associative_scan(combine, (a, b), axis=1)
    return h.astype(xr.dtype)

def _chunk_attention(q, k, v, rel_bias):
    B, S, _ = q.shape
    nc = S // CHUNK
    band = BAND_CHUNKS * CHUNK

    def split(t):
        return t.reshape(B, nc, CHUNK, ATT_HEADS, ATT_HEAD_DIM)

    q, k, v = split(q), split(k), split(v)
    pad = ((0, 0), (LEFT_CHUNKS, 0), (0, 0), (0, 0), (0, 0))
    kp, vp = jnp.pad(k, pad), jnp.pad(v, pad)
    k_band = jnp.concatenate([kp[:, j:j + nc] for j in range(BAND_CHUNKS)], axis=2)
    v_band = jnp.concatenate([vp[:, j:j + nc] for j in range(BAND_CHUNKS)], axis=2)
    s = jnp.einsum('bnqhd,bnkhd->bnhqk', q, k_band).astype(jnp.float32) * (ATT_HEAD_DIM ** -0.5)
    rel = LEFT_CHUNKS * CHUNK + np.arange(CHUNK)[:, None] - np.arange(band)[None, :]
    rel_idx = np.clip(rel, -REL_CLIP, REL_CLIP) + REL_CLIP
    bias = rel_bias[:, rel_idx].astype(jnp.float32)
    key_chunk = (np.arange(nc)[:, None] - LEFT_CHUNKS
                 + (np.arange(band) // CHUNK)[None, :])
    valid = key_chunk >= 0
    s = jnp.where(valid[None, :, None, None, :], s + bias[None, None], NEG_INF)
    p = jax.nn.softmax(s, axis=-1).astype(v.dtype)
    o = jnp.einsum('bnhqk,bnkhd->bnqhd', p, v_band)
    return o.reshape(B, S, ATT_WIDTH)

def _memory_cross_attention(h, mem_n, w_q, w_kv, w_o):
    B, S, D = h.shape
    M = mem_n.shape[1]
    q = (h @ w_q).reshape(B, S, MEM_HEADS, MEM_HEAD_DIM)
    kv = (mem_n @ w_kv).reshape(B, M, 2, MEM_HEADS, MEM_HEAD_DIM)
    k, v = kv[:, :, 0], kv[:, :, 1]
    s = jnp.einsum('bshd,bmhd->bhsm', q, k).astype(jnp.float32) * (MEM_HEAD_DIM ** -0.5)
    p = jax.nn.softmax(s, axis=-1).astype(h.dtype)
    o = jnp.einsum('bhsm,bmhd->bshd', p, v).reshape(B, S, D)
    return o @ w_o

def _peer(h, w_query, sub_keys, expert_u, expert_v):
    B, S, D = h.shape
    q = (h @ w_query).reshape(B, S, PEER_HEADS, 2, PEER_KEY_DIM)
    sc = jnp.einsum('bshpk,hpnk->bshpn', q, sub_keys).astype(jnp.float32)
    v1, i1 = lax.top_k(sc[..., 0, :], PEER_TOPK)
    v2, i2 = lax.top_k(sc[..., 1, :], PEER_TOPK)
    n_cand = PEER_TOPK * PEER_TOPK
    cand = (v1[..., :, None] + v2[..., None, :]).reshape(B, S, PEER_HEADS, n_cand)
    cand_idx = (i1[..., :, None] * N_KEYS + i2[..., None, :]).reshape(B, S, PEER_HEADS, n_cand)
    top_s, pos = lax.top_k(cand, PEER_TOPK)
    idx = jnp.take_along_axis(cand_idx, pos, axis=-1)
    g = jax.nn.softmax(top_s, axis=-1).astype(h.dtype)
    n_sel = PEER_HEADS * PEER_TOPK
    nb = (B * S) // PEER_BLOCK
    hb = h.reshape(nb, PEER_BLOCK, D)
    ib = idx.reshape(nb, PEER_BLOCK, n_sel)
    gb = g.reshape(nb, PEER_BLOCK, n_sel)

    def block(args):
        xt, it, gt = args
        u = expert_u[it]
        act = jax.nn.gelu(jnp.einsum('td,tkd->tk', xt, u))
        return jnp.einsum('tk,tkd->td', gt * act, expert_v[it])

    out = lax.map(block, (hb, ib, gb))
    return out.reshape(B, S, D)

def second_inputs(seed: int = 0) -> dict:
    key = jax.random.key(seed)
    ks = jax.random.split(key, 32)
    f32 = jnp.float32
    L = DEPTH_2

    def nrm(k, shape, scale):
        return jax.random.normal(k, shape, f32) * scale

    def gain(k, n):
        return 1.0 + 0.02 * jax.random.normal(k, (L, n), f32)

    a8 = jax.random.uniform(ks[10], (L, LRU_WIDTH), f32, 0.9, 0.999)
    s = a8 ** (1.0 / LRU_C)
    lru_lambda = jnp.log(s) - jnp.log1p(-s)
    return {
        "x": nrm(ks[0], (BATCH, SEQ, D_MODEL), 1.0),
        "mem": nrm(ks[1], (BATCH, MEM_LEN, D_MODEL), 1.0),
        "norm_mix": gain(ks[2], D_MODEL),
        "w_in": nrm(ks[3], (L, D_MODEL, IN_WIDTH), D_MODEL ** -0.5),
        "conv_w": nrm(ks[4], (L, CONV_WIDTH, LRU_WIDTH), CONV_WIDTH ** -0.5),
        "conv_b": nrm(ks[5], (L, LRU_WIDTH), 0.01),
        "gate_a_w": nrm(ks[6], (L, LRU_BLOCKS, LRU_BLOCK, LRU_BLOCK), LRU_BLOCK ** -0.5),
        "gate_a_b": nrm(ks[7], (L, LRU_WIDTH), 0.01),
        "gate_x_w": nrm(ks[8], (L, LRU_BLOCKS, LRU_BLOCK, LRU_BLOCK), LRU_BLOCK ** -0.5),
        "gate_x_b": nrm(ks[9], (L, LRU_WIDTH), 0.01),
        "lru_lambda": lru_lambda,
        "rel_bias": nrm(ks[11], (L, ATT_HEADS, 2 * REL_CLIP + 1), 0.5),
        "norm_grp_a": gain(ks[12], LRU_WIDTH),
        "norm_grp_b": gain(ks[13], ATT_WIDTH),
        "w_out": nrm(ks[14], (L, MIX_WIDTH, D_MODEL), MIX_WIDTH ** -0.5),
        "norm_cross": gain(ks[15], D_MODEL),
        "norm_mem": gain(ks[16], D_MODEL),
        "w_q_mem": nrm(ks[17], (L, D_MODEL, D_MODEL), D_MODEL ** -0.5),
        "w_kv_mem": nrm(ks[18], (L, D_MODEL, 2 * D_MODEL), D_MODEL ** -0.5),
        "w_o_mem": nrm(ks[19], (L, D_MODEL, D_MODEL), D_MODEL ** -0.5),
        "norm_ffn": gain(ks[20], D_MODEL),
        "w_query": nrm(ks[21], (L, D_MODEL, PEER_HEADS * PEER_QUERY_DIM), D_MODEL ** -0.5),
        "sub_keys": nrm(ks[22], (L, PEER_HEADS, 2, N_KEYS, PEER_KEY_DIM), PEER_KEY_DIM ** -0.5),
        "expert_u": nrm(ks[23], (L, N_EXPERTS, D_MODEL), D_MODEL ** -0.5),
        "expert_v": nrm(ks[24], (L, N_EXPERTS, D_MODEL), PEER_HEADS ** -0.5),
        "norm_final": 1.0 + 0.02 * jax.random.normal(ks[25], (D_MODEL,), f32),
    }

def second_block(x, mem, norm_mix, w_in, conv_w, conv_b, gate_a_w, gate_a_b, gate_x_w, gate_x_b,
              lru_lambda, rel_bias, norm_grp_a, norm_grp_b, w_out, norm_cross, norm_mem,
              w_q_mem, w_kv_mem, w_o_mem, norm_ffn, w_query, sub_keys, expert_u, expert_v,
              norm_final):
    splits = [LRU_WIDTH, 2 * LRU_WIDTH, 2 * LRU_WIDTH + ATT_WIDTH, 2 * LRU_WIDTH + 2 * ATT_WIDTH]
    for l in range(DEPTH_2):
        hn = _rmsnorm(x, norm_mix[l])
        z = hn @ w_in[l]
        x_lru, gate, q, k, v = jnp.split(z, splits, axis=-1)
        y_a = _rg_lru(x_lru, conv_w[l], conv_b[l], gate_a_w[l], gate_a_b[l],
                      gate_x_w[l], gate_x_b[l], lru_lambda[l]) * jax.nn.gelu(gate)
        y_b = _chunk_attention(q, k, v, rel_bias[l])
        y = jnp.concatenate([_rmsnorm(y_a, norm_grp_a[l]), _rmsnorm(y_b, norm_grp_b[l])], axis=-1)
        x = x + y @ w_out[l]
        x = x + _memory_cross_attention(_rmsnorm(x, norm_cross[l]), _rmsnorm(mem, norm_mem[l]),
                                        w_q_mem[l], w_kv_mem[l], w_o_mem[l])
        x = x + _peer(_rmsnorm(x, norm_ffn[l]), w_query[l], sub_keys[l], expert_u[l], expert_v[l])
    return _rmsnorm(x, norm_final)


def setup_inputs(seed=0):
    out = dict(first_inputs(seed))
    for name, value in second_inputs(seed + 1).items():
        if name != "x":
            out[name + "_2"] = value
    return out


def reference(
    x, c, positions, ada_w, ada_b, norm_mix, norm_mlp, mlp_w1, mlp_w2, mla_w_in, mla_g_qa,
    mla_w_qb, mla_g_kva, mla_w_kvb, mla_g_q, mla_g_k, mla_w_o, dil_w_in, dil_g_q, dil_g_k,
    dil_w_o, rel_bias, mem_2, norm_mix_2, w_in_2, conv_w_2, conv_b_2, gate_a_w_2, gate_a_b_2,
    gate_x_w_2, gate_x_b_2, lru_lambda_2, rel_bias_2, norm_grp_a_2, norm_grp_b_2, w_out_2,
    norm_cross_2, norm_mem_2, w_q_mem_2, w_kv_mem_2, w_o_mem_2, norm_ffn_2, w_query_2,
    sub_keys_2, expert_u_2, expert_v_2, norm_final_2,
):
    x = first_block(
        x, c, positions, ada_w, ada_b, norm_mix, norm_mlp, mlp_w1, mlp_w2, mla_w_in, mla_g_qa,
        mla_w_qb, mla_g_kva, mla_w_kvb, mla_g_q, mla_g_k, mla_w_o, dil_w_in, dil_g_q, dil_g_k,
        dil_w_o, rel_bias,
    )
    return second_block(
        x, mem_2, norm_mix_2, w_in_2, conv_w_2, conv_b_2, gate_a_w_2, gate_a_b_2, gate_x_w_2,
        gate_x_b_2, lru_lambda_2, rel_bias_2, norm_grp_a_2, norm_grp_b_2, w_out_2, norm_cross_2,
        norm_mem_2, w_q_mem_2, w_kv_mem_2, w_o_mem_2, norm_ffn_2, w_query_2, sub_keys_2,
        expert_u_2, expert_v_2, norm_final_2,
    )


_drawn_inputs = setup_inputs


def setup_inputs(seed=0):
    import zlib

    import numpy as np

    out = dict(_drawn_inputs(seed))
    spreads = {}
    factors = {'norm_mix': 4.784,
     'mla_g_qa': 8.0,
     'mla_g_kva': 3.97,
     'mla_g_q': 8.0,
     'mla_g_k': 8.0,
     'dil_g_q': 8.0,
     'dil_g_k': 8.0,
     'rel_bias': 2.779,
     'conv_b_2': 2.688,
     'gate_a_b_2': 8.0,
     'gate_x_b_2': 8.0,
     'norm_grp_a_2': 3.547,
     'norm_grp_b_2': 3.643,
     'norm_cross_2': 8.0,
     'norm_mem_2': 8.0,
     'norm_ffn_2': 23.756,
     'norm_final_2': 7.937}
    for name, (base, spread) in spreads.items():
        noise = np.random.default_rng([zlib.crc32(name.encode()), seed]).standard_normal(out[name].shape)
        drawn = base * np.exp(spread * noise) if base else spread * noise
        out[name] = jnp.asarray(drawn.astype(out[name].dtype))
    for name, factor in factors.items():
        out[name] = (out[name] * factor).astype(out[name].dtype)
    return out
```

```python
from contextlib import ExitStack

import numpy as np
import concourse.bass as bass
from concourse import mybir

ALU = mybir.AluOpType
ACT = mybir.ActivationFunctionType
F32 = mybir.dt.float32
I32 = mybir.dt.int32
U32 = mybir.dt.uint32
AX = mybir.AxisListType

UNIT = 1024
NRAW = 4
NSPLIT = 3
F32R = mybir.dt.float32r
NEG = -1e30
MAGIC = 12582912.0
TWO_PI_A = 6.28125
TWO_PI_B = float(np.float32(2 * np.pi - 6.28125))
TWO_PI_C = float(2 * np.pi - 6.28125 - np.float64(np.float32(2 * np.pi - 6.28125)))

VEC = {}
_at = 0
for _name, _n in [("norm_mix", 16), ("norm_mlp", 16), ("ada_b", 96), ("g_qa", 3), ("g_kva", 2),
                  ("g_q", 1), ("g_k", 1), ("dil_g_q", 3), ("dil_g_k", 3), ("norm_mix_2", 8), ("conv_w", 16),
                  ("conv_b", 4), ("gate_a_b", 4), ("gate_x_b", 4), ("lam", 4), ("grp_a", 4), ("grp_b", 4),
                  ("cross", 8), ("memn", 8), ("ffn", 8)]:
    VEC[_name] = (_at, _n)
    _at += _n
NVEC = _at

CON = {}
_at = 0
for _name, _n in [("ident", 128), ("ones", 128), ("blk", 128), ("invf", 16), ("lo", 1), ("eps", 1), ("iota", 128)]:
    CON[_name] = (_at, _n)
    _at += _n
NCON = _at


class Queue:

    def __init__(self, name):
        self.name, self.items, self.count = name, [], 0

    def __call__(self, fn, *waits, mark=True):
        self.items.append((fn, flat(waits), (self.name, 1) if mark else None))
        if mark:
            self.count += 1
            return (self.name, self.count)

    def dma(self, fn, sem, value, *waits):
        self.items.append((fn, flat(waits), (sem, 16)))
        return (sem, value)

    def join(self, *waits):
        self.items.append((None, flat(waits), None))

    @property
    def last(self):
        return (self.name, self.count)


def flat(waits):
    out = []
    for w in waits:
        if w is None:
            continue
        if isinstance(w, tuple) and len(w) == 2 and isinstance(w[0], str):
            out.append(w)
        else:
            out += flat(w)
    return out


class Slots:

    def __init__(self, ids):
        self.free = [(i, []) for i in ids]

    def take(self):
        return self.free.pop(0)

    def give(self, i, *marks):
        self.free.append((i, flat(marks)))


def program(nc, d, out):
    plan = []
    build(nc, d, out, plan, True)
    build(nc, d, out, plan, False)


def build(nc, d, out, plan, dry):
    ctx = ExitStack()
    V, A, P, G, S = Queue("V"), Queue("A"), Queue("P"), Queue("G"), Queue("S")
    ve, ac, pe, gp, sy = nc.vector, nc.scalar, nc.tensor, nc.gpsimd, nc.sync
    count = [0]

    def sb(name, cols, dt=F32, where=None):
        count[0] += 1
        return (where or ctx).enter_context(nc.sbuf_tensor(f"{name}_{'d' if dry else 'r'}{count[0]}", [128, cols], dt))

    xT = sb("xT", 2048)
    vec = sb("vec", NVEC)
    con = sb("con", NCON)
    raw = [sb("raw", UNIT) for _ in range(NRAW)]
    wh = [sb("wh", UNIT, F32R) for _ in range(NSPLIT)]
    wl = [sb("wl", UNIT, F32R) for _ in range(NSPLIT)]
    mod = sb("mod", 96)
    col = sb("col", 64)
    psum = ctx.enter_context(nc.psum_tensor("psum" + ("d" if dry else "r"), [128, 8, 512], F32))

    banks = Slots(range(8))
    sem_uses = {}
    scope = [ExitStack()]
    lent = ExitStack()
    cond = sb("cond", UNIT, where=lent)
    araw = [sb("araw", UNIT, where=lent) for _ in range(2)]
    afree = Slots(range(2))

    def cc(name, i=0, n=None):
        a, m = CON[name]
        return con[:, a + i:a + i + (m if n is None else n)]

    def vc(name, i, n=1):
        a, m = VEC[name]
        return vec[:, a + i:a + i + n]

    ident, ones, blk = cc("ident"), cc("ones"), cc("blk")
    eps = cc("eps")

    def carve(cols, dt=F32):
        return sb("t", cols, dt, scope[0])[:]

    def phase(*more):
        scope[0].close()
        for m in more:
            m.close()
        scope[0] = ExitStack()
        done = [V.last, A.last, P.last, G.last]
        for q in (V, A, P, G):
            q.join(done)

    def sem_dma(q, eng, sem, dst, src, *waits):
        sem_uses[sem] = sem_uses.get(sem, 0) + 1
        return q.dma(lambda: eng.dma_start(dst, src), sem, 16 * sem_uses[sem], waits)

    rawfree, splitfree = Slots(range(NRAW)), Slots(range(NSPLIT))
    loaded, ready = {}, {}
    at = dict(load=0, split=0, get=0, hold=0)

    def pump():
        while at["load"] < len(plan) and len(rawfree.free) > at["hold"]:
            name, blk, n, kind = plan[at["load"]]
            i, marks = rawfree.take()
            loaded[at["load"]] = (i, sem_dma(S, sy, f"w{i}", raw[i][:, 0:n], d[name][blk][:, 0:n], marks))
            at["load"] += 1

    def split_ahead(upto):
        while at["split"] < min(upto, len(plan)) and at["split"] in loaded:
            name, blk, n, kind = plan[at["split"]]
            if kind == "split":
                if not splitfree.free:
                    break
                i, m = loaded.pop(at["split"])
                j, fr = splitfree.take()
                mh = act(wh[j][:, 0:n], raw[i][:, 0:n], ACT.Copy, m, fr)
                ml = tt(wl[j][:, 0:n], raw[i][:, 0:n], wh[j][:, 0:n].bitcast(F32), ALU.subtract, m, mh, fr)
                rawfree.give(i, ml)
                ready[at["split"]] = (j, ml)
            at["split"] += 1
            pump()

    def get(name, blk, n, kind="split"):
        k = at["get"]
        at["get"] += 1
        if dry:
            plan.append((name, blk, n, kind))
        assert plan[k] == (name, blk, n, kind)
        pump()
        split_ahead(k + NSPLIT + 4)
        if kind == "raw":
            return loaded.pop(k)
        return ready.pop(k)

    def put(j, mark):
        splitfree.give(j, mark)

    def mm3(o, l, r, start, stop, *waits, mark=False, loose=False):
        mm(o, l[0], r[0], start, False, waits, loose=loose)
        mm(o, l[0], r[1], False, False, loose=loose)
        return mm(o, l[1], r[0], False, stop, mark=mark, loose=loose)

    def mm(o, l, r, start, stop, *waits, mark=False, loose=False):
        return P(lambda: pe.matmul(o, l, r, start=start, stop=stop, skip_group_check=loose), *waits, mark=mark)

    def tr(o, i, *waits, mark=False):
        return P(lambda: pe.transpose(o, i, ident), *waits, mark=mark)

    def act(o, i, f, *waits, **kw):
        return A(lambda: ac.activation(o, i, f, **kw), *waits)

    def tt(o, a, b, op, *waits, q=None):
        q, e = (V, ve) if q is None else (G, gp)
        return q(lambda: e.tensor_tensor(o, a, b, op), *waits)

    def ts(o, a, s1, s2, op0, op1, *waits):
        if op1 is None:
            return V(lambda: ve.tensor_scalar(o, a, s1, None, op0), *waits)
        return V(lambda: ve.tensor_scalar(o, a, s1, s2, op0, op1), *waits)

    def stt(o, a, s, b, op0, op1, *waits):
        return V(lambda: ve.scalar_tensor_tensor(out=o, in0=a, scalar=s, in1=b, op0=op0, op1=op1), *waits)

    def gts(o, a, s1, s2, op0, op1, *waits):
        if op1 is None:
            return G(lambda: gp.tensor_scalar(o, a, s1, None, op0), *waits)
        return G(lambda: gp.tensor_scalar(o, a, s1, s2, op0, op1), *waits)

    def recip(o, a, *waits):
        return V(lambda: ve.reciprocal(o, a), *waits)

    def cp(o, a, *waits):
        return V(lambda: ve.tensor_copy(o, a), *waits)

    def red(o, a, op, *waits):
        return V(lambda: ve.tensor_reduce(o, a, AX.X, op), *waits)

    def fill(o, v, *waits):
        return V(lambda: ve.memset(o, v), *waits)

    def ttr(o, a, b, op0, op1, init, acc, *waits):
        return V(lambda: ve.tensor_tensor_reduce(out=o, in0=a, in1=b, scale=1.0, scalar=init, op0=op0, op1=op1,
                                                 accum_out=acc), *waits)

    def scan(o, a, b, *waits):
        return V(lambda: ve.tensor_tensor_scan(o, a, b, 0.0, ALU.mult, ALU.add), *waits)

    def rsqrt(o, src, scale, x, y, *waits):
        m1 = act(x, src, ACT.Identity, waits, scale=scale, bias=eps)
        m2 = act(y, x, ACT.Abs_reciprocal_sqrt, m1)
        m = tt(o, y, y, ALU.mult, m2)
        m = stt(o, x, -0.5, o, ALU.mult, ALU.mult, m)
        return m1, stt(o, o, 1.5, y, ALU.add, ALU.mult, m)

    def bank():
        i, marks = banks.take()
        return i, psum[:, i, :], marks

    m_con = sem_dma(A, ac, "c0", con[:], d["con"])
    m_vec = sem_dma(A, ac, "c1", vec[:], d["vec"])
    m_x = sem_dma(S, sy, "c2", xT[:], d["xT"])
    m_cond = act(cond[:], cond[:], ACT.Silu, sem_dma(A, ac, "c12", cond[:], d["c_row"]))
    P.join(m_con, m_vec)
    V.join(m_con, m_vec, m_x)
    A.join(m_con, m_vec, m_x)
    G.join(m_con)

    def ada(layer, lo, n):
        base = 48 * layer + lo
        q = []
        for c in range(n + 2):
            if c >= 2:
                i, mw = q.pop(0)
                u = araw[i][:]
                last = ttr(u, u, cond[:], ALU.mult, ALU.add, 0.0, mod[:, base + c - 2:base + c - 1], mw, m_cond)
                afree.give(i, last)
            if c < n:
                i, marks = afree.take()
                q.append((i, sem_dma(G, gp, f"a{i}", araw[i][:], d["ada_w"][base + c], marks)))
            yield
        m_mod[0] = tt(mod[:, base:base + n], mod[:, base:base + n], vc("ada_b", base, n), ALU.add, last)
        yield

    side2, m_mod = [], [None]

    def tick2():
        if side2:
            try:
                next(side2[0])
            except StopIteration:
                side2.pop(0)

    def drain2():
        while side2:
            tick2()
        V.join(m_mod[0])

    side, pend, every = [], [], [1, 0]

    def flush(age=0):
        while pend and pend[0][0] >= age:
            pend.pop(0)[1]()

    def tick():
        flush(1)
        for x in pend:
            x[0] += 1
        every[1] += 1
        if every[1] % every[0] == 0:
            tick2()
        step_side()

    def step_side():
        if side:
            try:
                next(side[0])
            except StopIteration:
                side.pop(0)
                step_side()

    def drain_side():
        while side:
            step_side()

    def chain(*gens):
        for g in gens:
            yield from g

    def norm_a(src, nk, *waits, sq=None, tmp=None):
        half = nk * 128
        s3 = src.rearrange("p (k t) -> p k t", k=nk)
        q3 = sq.rearrange("p (k t) -> p k t", k=nk)
        m1 = act(sq[:, 0:half], src[:, 0:half], ACT.Square, waits)
        m2 = act(sq[:, half:2 * half], src[:, half:2 * half], ACT.Square)
        b, ps, fr = bank()
        for k in range(nk):
            m = mm(ps[:, 0:256], ones, q3[:, k, :], k == 0, k == nk - 1, fr, m1 if k < nk // 2 else m2,
                   mark=k == nk - 1)
        tmp = carve(768) if tmp is None else tmp
        rs = tmp[:, 0:256]
        m0, m = rsqrt(rs, ps[:, 0:256], 1.0 / (nk * 128), tmp[:, 256:512], tmp[:, 512:768], m)
        banks.give(b, m0)
        return [tt(q3[:, k0:k0 + nk // 2, :], s3[:, k0:k0 + nk // 2, :],
                   rs.unsqueeze(1).broadcast_to([128, nk // 2, 256]), ALU.mult, m) for k0 in (0, nk // 2)]

    def norm_b(nk, gain, shift, dst, ms, *waits, sq=None):
        outs, late = [], None
        for k in range(nk):
            z = slice(k * 256, k * 256 + 256)
            m = ms[k // (nk // 2)]
            if shift is None:
                m2 = ts(sq[:, z], sq[:, z], gain(k), None, ALU.mult, None, m, waits)
            else:
                m2 = ts(sq[:, z], sq[:, z], gain(k), shift(k), ALU.mult, ALU.add, m, waits)
            m3 = act(dst[0][:, z], sq[:, z], ACT.Copy, m2)
            if late:
                outs.append(tt(dst[1][:, late[0]], sq[:, late[0]], dst[0][:, late[0]].bitcast(F32), ALU.subtract,
                               late[1]))
            late = (z, [m2, m3])
        outs.append(tt(dst[1][:, late[0]], sq[:, late[0]], dst[0][:, late[0]].bitcast(F32), ALU.subtract, late[1]))
        return outs

    def norm(src, nk, gain, shift, dst, *waits, sq=None, tmp=None):
        ms = norm_a(src, nk, waits, sq=sq, tmp=tmp)
        return norm_b(nk, gain, shift, dst, ms, waits, sq=sq)

    def sp(pair, k, n=256, a=0, w=None):
        return [x[:, k * n + a:k * n + a + (n - a if w is None else w)] for x in pair]

    def wsp(j, a, n):
        return [wh[j][:, a:a + n], wl[j][:, a:a + n]]

    def project(name, n, src, nk, srcm, done, first=0, own=None):
        for c in range(n // 128):
            j, mw = get(name, first + c, nk * 128)
            if c % 2 == 0:
                b, ps, fr = bank()
                P.join(fr)
            P.join(mw)
            o = ps[:, (c % 2) * 256:(c % 2) * 256 + 256]
            for k in range(nk):
                last = mm3(o, wsp(j, k * 128, 128), sp(src, k), k == 0, k == nk - 1, srcm[k] if c == 0 else None,
                           mark=k == nk - 1)
            put(j, last)
            if c % 2:
                m = done(c // 2, ps, last)
                if own:
                    own[0](m, b)
                else:
                    banks.give(b, m)
            tick()

    def tok_units(name, first, src, srcm, width):
        b, ps, fr = bank()
        P.join(fr)
        for e in range(2):
            j, mw = get(name, first + e, 4 * width)
            P.join(mw)
            for t in range(2):
                for k in range(4):
                    last = mm3(ps[:, t * width:(t + 1) * width], sp(src, 4 * e + k, 256, t * 128, 128),
                               wsp(j, k * width, width), e == 0 and t == 0 and k == 0, e == 1 and t == 1 and k == 3,
                               srcm[4 * e + k], mark=t == 1 and k == 3, loose=True)
            put(j, last)
            tick()
        return b, ps, last

    def project_tok(name, n, src, srcm, dst, first=0):
        out = []
        d3 = dst.rearrange("p (t n) -> p t n", t=2)
        for c2 in range(n // 256):
            b, ps, last = tok_units(name, first + 2 * c2, src, srcm, 256)
            m = act(d3[:, :, c2 * 256:c2 * 256 + 256], ps.rearrange("p (t n) -> p t n", t=2), ACT.Copy, last)
            banks.give(b, m)
            out.append(m)
        return out

    def to_feature(src3, nk, width, dst, srcm, gain=None, split=False):
        outs = []
        for c0 in range(0, nk, 2):
            n = min(2, nk - c0)
            b, ps, fr = bank()
            P.join(fr, srcm)
            for c in range(n):
                for t in range(2):
                    last = tr(ps[0:width, c * 256 + t * 128:c * 256 + t * 128 + 128],
                              src3[:, t, (c0 + c) * width:(c0 + c + 1) * width], mark=(c == n - 1 and t == 1))
            z = slice(c0 * 256, (c0 + n) * 256)
            if split and gain is None:
                m = act(dst[0][:, z], ps[:, 0:n * 256], ACT.Copy, last)
                m = tt(dst[1][:, z], ps[:, 0:n * 256], dst[0][:, z].bitcast(F32), ALU.subtract, m)
                outs += [m] * n
            elif split:
                for c in range(n):
                    y = slice((c0 + c) * 256, (c0 + c + 1) * 256)
                    m1 = act(dst[0][:, y], ps[:, c * 256:c * 256 + 256], ACT.Copy, last, scale=gain(c0 + c))
                    last = m1
                for c in range(n):
                    y = slice((c0 + c) * 256, (c0 + c + 1) * 256)
                    m = stt(dst[1][:, y], ps[:, c * 256:c * 256 + 256], gain(c0 + c), dst[0][:, y].bitcast(F32),
                            ALU.mult, ALU.subtract, m1)
                    outs.append(m)
            elif gain is None:
                m = cp(dst[0:width, c0:c0 + n, :], ps[0:width, 0:n * 256].rearrange("p (c t) -> p c t", c=n), last)
                outs += [m] * n
            else:
                for c in range(n):
                    m = ts(dst[0:width, c0 + c, :], ps[0:width, c * 256:c * 256 + 256], gain(c0 + c), None, ALU.mult,
                           None, last)
                    outs.append(m)
            banks.give(b, m)
        return outs

    total = {}

    def squares(c2, m, ring, now=False):
        if c2 == 0:
            total["bank"] = bank()
            total["free"] = [None, None]
        r = ring[:, (c2 % 2) * 512:(c2 % 2) * 512 + 512]
        m = act(r, xT[:, c2 * 512:c2 * 512 + 512], ACT.Square, m, total["free"][c2 % 2])
        if c2 == 2:
            act(col[:, 60:61], eps, ACT.Abs_reciprocal_sqrt, m)

        def sums():
            P.join(m, total["bank"][2])
            for j in range(2):
                last = mm(total["bank"][1][:, 0:256], ones, r[:, j * 256:j * 256 + 256], c2 == 0 and j == 0,
                          c2 == 3 and j == 1, mark=j == 1)
            total["free"][c2 % 2] = total["last"] = last

        if now:
            sums()
        else:
            flush()
            pend.append([0, sums])

    def norm_x(gain, shift, dst, *waits, sq=None, tmp=None):
        flush()
        b, ps, _ = total["bank"]
        m0, m = rsqrt(tmp[:, 0:256], ps[:, 0:256], 1.0 / 1024, tmp[:, 256:512], tmp[:, 512:768], total["last"])
        banks.give(b, m0)
        outs = []

        def low(k, m1, m2):
            z = slice(k * 256, k * 256 + 256)
            if shift is None:
                outs.append(tt(dst[1][:, z], sq[:, z], dst[0][:, z].bitcast(F32), ALU.subtract, m1, m2,
                               q=G if k % 2 else None))
            else:
                outs.append(stt(dst[1][:, z], sq[:, z], shift(k), dst[0][:, z].bitcast(F32), ALU.add, ALU.subtract,
                                m1, m2))

        late = None
        for k in range(8):
            z = slice(k * 256, k * 256 + 256)
            m1 = stt(sq[:, z], xT[:, z], gain(k), tmp[:, 0:256], ALU.mult, ALU.mult, m, waits)
            if shift is None:
                m2 = act(dst[0][:, z], sq[:, z], ACT.Copy, m1)
            else:
                m2 = act(dst[0][:, z], sq[:, z], ACT.Identity, m1, bias=shift(k))
            if late:
                low(*late)
            late = (k, m1, m2)
        low(*late)
        return outs

    def residual(gate, ring):
        def done(c2, ps, last):
            for j in range(2):
                c = 2 * c2 + j
                xs = xT[:, c * 256:c * 256 + 256]
                if gate is None:
                    m = tt(xs, ps[:, j * 256:j * 256 + 256], xs, ALU.add, last)
                else:
                    m = stt(xs, ps[:, j * 256:j * 256 + 256], gate(c), xs, ALU.mult, ALU.add, last)
            squares(c2, m, ring)
            return m
        return done

    def attention(nh, scores, bias, scale, vals, dv, out, waits, work=None):
        NB = 3
        work = carve(NB * 1024) if work is None else work
        sbuf = work[:, 0:NB * 512].rearrange("p (b n) -> p b n", b=NB)
        ptb = work[:, NB * 512:NB * 1024].rearrange("p (b n) -> p b n", b=NB)
        st = carve(8 * nh).rearrange("p (s h t) -> p s h t", s=4, h=nh)
        sfree, pfree = Slots(range(NB)), Slots(range(NB))
        hold = {}
        per = 256 // dv
        acc, outs = {}, []

        def s1(h):
            b, ps, fr = bank()
            P.join(fr, waits(h) if callable(waits) else waits if h == 0 else None)
            m = scores(h, ps)
            i, sf = sfree.take()
            sv = sbuf[:, i, :]
            if bias is None:
                m = red(st[:, 0, h, :], ps.rearrange("p (t n) -> p t n", t=2), ALU.max, m)
                src = ps
            else:
                for t in range(2):
                    m = ttr(sv[:, t * 256:t * 256 + 256], ps[:, t * 256:t * 256 + 256], bias[:, h, t, :], ALU.add,
                            ALU.max, -3e38, st[:, 0, h, t:t + 1], m, sf)
                src = sv
            m = ts(st[:, 1, h, :], st[:, 0, h, :], -scale, None, ALU.mult, None, m)
            for t in range(2):
                m = act(sv[:, t * 256:t * 256 + 256], src[:, t * 256:t * 256 + 256], ACT.Exp, m, sf,
                        bias=st[:, 1, h, t:t + 1], scale=scale, accum_out=st[:, 2, h, t:t + 1])
            banks.give(b, m)
            hold[h] = (i, m)

        def s1b(h):
            i, m = hold[h]
            m = recip(st[:, 3, h, :], st[:, 2, h, :], m)
            for t in range(2):
                z = sbuf[:, i, t * 256:t * 256 + 256]
                m2 = ts(z, z, st[:, 3, h, t:t + 1], None, ALU.mult, None, m)
            hold[h] = (i, m2)

        def s2(h):
            i, m = hold[h]
            b, ps, fr = bank()
            P.join(fr, m)
            for kb in range(2):
                for t in range(2):
                    last = tr(ps[:, (2 * kb + t) * 128:(2 * kb + t) * 128 + 128],
                              sbuf[:, i, t * 256 + kb * 128:t * 256 + kb * 128 + 128], mark=(kb == 1 and t == 1))
            sfree.give(i, last)
            j, pf = pfree.take()
            m = act(ptb[:, j, :], ps, ACT.Copy, last, pf)
            banks.give(b, m)
            hold[h] = (j, m)

        def s3(h):
            j, m = hold.pop(h)
            g = h % per
            if g == 0:
                acc[0] = bank()
                P.join(acc[0][2])
            b, ps, fr = acc[0]
            P.join(m)
            w = min(dv, 128)
            for e in range(dv // w):
                r, c = divmod(g * dv + e * w, 128)[::-1]
                for kb in range(2):
                    last = mm(ps[r:r + w, c * 256:c * 256 + 256], vals(h, kb)[:, e * w:(e + 1) * w],
                              ptb[:, j, kb * 256:kb * 256 + 256], kb == 0, kb == 1, mark=kb == 1)
            pfree.give(j, last)
            if g == per - 1:
                m = out(h // per, ps, last)
                banks.give(b, m)
                outs.extend([m, m])

        for n in range(nh + 3):
            if n < nh:
                s1(n)
            if 0 <= n - 1 < nh:
                s1b(n - 1)
            if 0 <= n - 2 < nh:
                s2(n - 2)
            if 0 <= n - 3 < nh:
                s3(n - 3)
            tick()
        return outs

    def split_out(dst):
        def out(c2, ps, last):
            z = slice(c2 * 512, c2 * 512 + 512)
            m = act(dst[0][:, z], ps, ACT.Copy, last)
            return tt(dst[1][:, z], ps, dst[0][:, z].bitcast(F32), ALU.subtract, m)
        return out

    xs3 = xT[:].rearrange("p (k t) -> p k t", k=8)

    def mod_cols(layer, part, g):
        base = 48 * layer
        o = col[:, 8 * (2 * layer + (part > 0)):8 * (2 * layer + (part > 0)) + 8]
        sc = mod[:, base + 8 * (part + 1):base + 8 * (part + 2)]
        sh = base + 8 * part
        m = stt(o, sc, 1.0, g, ALU.add, ALU.mult, V.last)
        return m, (lambda k: o[:, k:k + 1]), (lambda k: mod[:, sh + k:sh + k + 1])

    phase()
    na = carve(2048)
    hh = [carve(2048, F32R), carve(2048, F32R)]
    ntmp = carve(768)
    keep, scope[0] = scope[0], ExitStack()
    first = carve(16 * UNIT)
    early = []
    pump()
    for e in range(8):
        early.append(sem_dma(S, sy, f"e{e}", first[:, e * 2048:(e + 1) * 2048].rearrange("p (u n) -> p u n", u=2),
                             d["ada_w"][2 * e:2 * e + 2].rearrange("u p n -> p u n")))
    for c in [0, 1, 3, 4, 2] + list(range(5, 16)):
        if c == 2:
            ms = norm_a(xT[:], 8, m_x, sq=na, tmp=ntmp)
            split_ahead(NSPLIT)
        u, mw = first[:, c * UNIT:(c + 1) * UNIT], early[c // 2]
        if c in (2, 5, 8, 10, 12):
            last = act(u, u, ACT.Copy, tt(u, u, cond[:], ALU.mult, mw, m_cond, q=G), accum_out=mod[:, c:c + 1])
        else:
            m = ttr(u, u, cond[:], ALU.mult, ALU.add, 0.0, mod[:, c:c + 1], mw, m_cond)
    m = tt(mod[:, 0:16], mod[:, 0:16], vc("ada_b", 0, 16), ALU.add, last, m)
    m, gn, sf = mod_cols(0, 0, vc("norm_mix", 0, 8))
    hm = norm_b(8, gn, sf, hh, ms, m, sq=na)
    scope[0].close()
    scope[0] = keep
    for q in (A, V, G):
        q.join(last, m)
    side2.append(chain(ada(0, 16, 8), ada(0, 24, 16)))

    lat = carve(2 * 672).rearrange("p (t n) -> p t n", t=2)
    lm = []
    for s, width in enumerate((256, 256, 160)):
        b, ps, last = tok_units("mla_w_in", 2 * s, hh, hm, width)
        m = act(lat[:, :, s * 256:s * 256 + width], ps[:, 0:2 * width].rearrange("p (t n) -> p t n", t=2), ACT.Copy,
                last)
        lm.append(m)
        banks.give(b, m)

    junk = ntmp
    ss = carve(16)
    for t in range(2):
        for j, (a, n) in enumerate(((0, 384), (384, 256))):
            m = act(junk[:, 0:n], lat[:, t, a:a + n], ACT.Square, lm, A.last, scale=float(n) ** -0.5,
                    accum_out=ss[:, 2 * t + j:2 * t + j + 1])
    m = act(ss[:, 4:8], ss[:, 0:4], ACT.Sqrt, m, bias=eps)
    m = recip(ss[:, 8:12], ss[:, 4:8], m)
    latn = carve(2 * 640).rearrange("p (t n) -> p t n", t=2)
    for t in range(2):
        for j, (a, n) in enumerate(((0, 384), (384, 256))):
            m2 = ts(latn[:, t, a:a + n], lat[:, t, a:a + n], ss[:, 8 + 2 * t + j:9 + 2 * t + j], None, ALU.mult, None, m)
    latT = [carve(5 * 256, F32R), carve(5 * 256, F32R)]
    tm = to_feature(latn, 5, 128, latT, m2, gain=lambda c: vc("g_qa", c) if c < 3 else vc("g_kva", c - 3), split=True)

    posI = carve(2, I32)
    pos = carve(2)
    mp = sem_dma(G, gp, "c3", posI, d["pos_col"])
    m = cp(pos, posI, mp)
    ang = carve(32).rearrange("p (t n) -> p t n", t=2)
    for t in range(2):
        m2 = ts(ang[:, t, :], cc("invf"), pos[:, t:t + 1], None, ALU.mult, None, m)
    trig = carve(64).rearrange("p (s t n) -> p s t n", s=2, t=2)
    kk = carve(64).rearrange("p (s t n) -> p s t n", s=2, t=2)
    for s in range(2):
        m = ts(kk[:, s], ang, float(1 / (2 * np.pi)), 0.25 * s, ALU.mult, ALU.add, m2)
        m = ts(kk[:, s], kk[:, s], MAGIC, None, ALU.add, None, m)
        m = ts(kk[:, s], kk[:, s], -MAGIC, None, ALU.add, None, m)
        m = stt(trig[:, s], kk[:, s], -TWO_PI_A, ang, ALU.mult, ALU.add, m)
        m = stt(trig[:, s], kk[:, s], -TWO_PI_B, trig[:, s], ALU.mult, ALU.add, m)
        m = stt(trig[:, s], kk[:, s], -TWO_PI_C, trig[:, s], ALU.mult, ALU.add, m)
        m = ts(trig[:, s], trig[:, s], float(np.pi / 2) * s, 3.1415925, ALU.add, ALU.min, m)
        m = ts(trig[:, s], trig[:, s], -3.1415925, None, ALU.max, None, m)
    m_trig = act(trig, trig, ACT.Sin, m)
    sin, cos = trig[:, 0], trig[:, 1]

    q_tok = carve(2 * 1536).rearrange("p (t n) -> p t n", t=2)
    qm = []
    for s in range(6):
        j, mw = get("mla_w_qb", s, 768)
        b, ps, fr = bank()
        P.join(fr, mw, tm[0:3])
        for t in range(2):
            for k in range(3):
                last = mm3(ps[:, t * 256:t * 256 + 256], sp(latT, k, 256, t * 128, 128), wsp(j, k * 256, 256),
                           k == 0, k == 2, mark=t == 1 and k == 2)
        put(j, last)
        m = act(q_tok[:, :, s * 256:s * 256 + 256], ps.rearrange("p (t n) -> p t n", t=2), ACT.Copy, last)
        banks.give(b, m)
        qm.append(m)
        tick()
    sqh = carve(3072)
    tmp = sqh[:, 0:4 * 512]

    def rope(dst1, dst2, x1, x2, cs, sn, shape, n, *waits):
        t = [tmp[:, j * 512:j * 512 + n].rearrange(shape[0], **shape[1]) for j in range(4)]
        m = [tt(t[0], x1, cs, ALU.mult, waits), tt(t[1], x2, sn, ALU.mult), tt(t[2], x2, cs, ALU.mult),
             tt(t[3], x1, sn, ALU.mult)]
        m1 = tt(dst1, t[0], t[1], ALU.subtract, m)
        return tt(dst2, t[2], t[3], ALU.add, m1)

    hs = carve(8 * 32)
    xn = {}

    qT = carve(16 * 256).rearrange("p (h t) -> p h t", h=16)
    kT = carve(16 * 256).rearrange("p (h t) -> p h t", h=16)
    sqk = kT.rearrange("p h t -> p (h t)")[:, 0:3072]

    sqs = {}

    def head_squares(key, x, dst, mx):
        sqs[key] = (x, dst, act(dst, x, ACT.Square, mx))

    def head_norms():
        ms, ns = {}, {}
        h = {key: [hs[:, 128 * e + 32 * z:128 * e + 32 * z + 32] for z in range(4)] for e, key in enumerate("qk")}
        for key in "qk":
            x, dst, m = sqs[key]
            ms[key] = red(h[key][0], dst.rearrange("p (h n) -> p h n", n=96), ALU.add, m)
        for key in "qk":
            _, ns[key] = rsqrt(h[key][2], h[key][0], 1.0 / 96, h[key][1], h[key][3], ms[key])
        for key in "qk":
            x4 = sqs[key][0].rearrange("p (t h n) -> p t h n", t=2, h=16)
            h3 = h[key][2].rearrange("p (t h) -> p t h", t=2).unsqueeze(3)
            for e in range(2):
                xn[key, e] = []
                for u, v, q in ((6, 8, G), (0, 6, None)):
                    u, v = 8 * e + u, 8 * e + v
                    z = x4[:, :, u:v, :]
                    xn[key, e].append(tt(z, z, h3[:, :, u:v].broadcast_to([128, 2, v - u, 96]), ALU.mult, ns[key],
                                         q=q))

    def q_side():
        q4 = q_tok.rearrange("p t (h n) -> p t h n", h=16)
        cb, sb_ = (z.unsqueeze(2).broadcast_to([128, 2, 16, 16]) for z in (cos, sin))
        mq = rope(q4[:, :, :, 64:80], q4[:, :, :, 80:96], q4[:, :, :, 64:80], q4[:, :, :, 80:96], cb, sb_,
                  ("p (t h n) -> p t h n", dict(t=2, h=16)), 512, qm, m_trig)
        yield
        head_squares("q", q_tok.rearrange("p t n -> p (t n)"), sqh, mq)
        yield

    kr = carve(64).rearrange("p (t n) -> p t n", t=2)
    mk = rope(kr[:, :, 0:16], kr[:, :, 16:32], lat[:, :, 640:656], lat[:, :, 656:672], cos, sin,
              ("p (t n) -> p t n", dict(t=2)), 32, lm, m_trig)
    side.append(q_side())
    k_tok = carve(2 * 1536).rearrange("p (t h n) -> p t h n", t=2, h=16)
    mk2 = [cp(k_tok[:, t, :, 64:96], kr[:, t, :].unsqueeze(1).broadcast_to([128, 16, 32]), mk) for t in range(2)]
    v_tok = carve(2 * 1024).rearrange("p (t h n) -> p t h n", t=2, h=16)
    km, vm = [], []
    for s in range(4):
        j, mw = get("mla_w_kvb", s, 1024)
        P.join(mw, tm[3:5])
        for t in range(2):
            b, ps, fr = bank()
            P.join(fr)
            for k in range(2):
                last = mm3(ps, sp(latT, 3 + k, 256, t * 128, 128), wsp(j, k * 512, 512), k == 0, k == 1, mark=k == 1)
            h0 = 4 * s
            p3 = ps.rearrange("p (h n) -> p h n", h=4)
            m = act(k_tok[:, t, h0:h0 + 4, 0:64], p3[:, :, 0:64], ACT.Copy, last)
            km.append(m)
            m2 = cp(v_tok[:, t, h0:h0 + 4, :], p3[:, :, 64:128], m)
            vm.append(m2)
            banks.give(b, m, m2)
        put(j, last)
        tick()

    drain_side()
    head_squares("k", k_tok.rearrange("p t h n -> p (t h n)"), sqk, [mk2, km])
    head_norms()
    gms = {}

    def turned(key, x3, dst, g):
        def one(c0):
            b, ps, fr = bank()
            P.join(fr, xn[key, c0 // 8])
            for c in range(2):
                for t in range(2):
                    last = tr(ps[0:96, c * 256 + t * 128:c * 256 + t * 128 + 128],
                              x3[:, t, (c0 + c) * 96:(c0 + c + 1) * 96], mark=c == 1 and t == 1)
            p3 = ps[0:96].rearrange("p (c t) -> p c t", c=2)
            if key == "q":
                m = act(dst[0:96, c0:c0 + 2, :], p3, ACT.Copy, last, scale=vc(g, 0)[0:96, :])
            else:
                m = ts(dst[0:96, c0:c0 + 2, :], p3, vc(g, 0)[0:96, :], None, ALU.mult, None, last)
            banks.give(b, m)
            gms[key, c0] = m
        return one

    tq = turned("q", q_tok, qT, "g_q")
    tk = turned("k", k_tok.rearrange("p t h n -> p t (h n)"), kT, "g_k")
    tq(0)
    tq(2)
    tk(0)
    tk(2)

    def mla_scores(h, ps):
        if h % 2 == 0 and h + 4 < 16:
            tq(h + 4)
            tk(h + 4)
        for t in range(2):
            m = mm(ps[:, t * 256:t * 256 + 256], qT[0:96, h, t * 128:t * 128 + 128], kT[0:96, h, :], True, True,
                   mark=t == 1)
        return m

    om = attention(16, mla_scores, None, 96.0 ** -0.5, lambda h, kb: v_tok[:, kb, h, :], 64, split_out(hh), 
                   lambda h: [gms["q", h & ~1], gms["k", h & ~1], vm if h == 0 else None],
                   work=sqh)
    drain2()
    project("mla_w_o", 1024, hh, 8, om, residual(lambda c: mod[:, 16 + c:17 + c], sqh))

    def mlp(layer, unpermute):
        phase()
        m, gn, sf = mod_cols(layer, 3, vc("norm_mlp", 8 * layer, 8))
        hh = [carve(2048, F32R), carve(2048, F32R)]
        sq = carve(2048)
        hm = norm_x(gn, sf, hh, m, sq=sq, tmp=carve(768))
        h1 = [carve(32 * 256, F32R), carve(32 * 256, F32R)]
        rb = carve(2 * 512).rearrange("p (b n) -> p b n", b=2)
        sb2 = carve(2 * 512).rearrange("p (b n) -> p b n", b=2)
        ms = {}

        def done(c2, ps, last):
            r, q = rb[:, c2 % 2, :], sb2[:, c2 % 2, :]
            m = act(r, ps, ACT.Relu, last, ms.get(c2 - 2))
            z = slice(c2 * 512, c2 * 512 + 512)
            mh = act(h1[0][:, z], r, ACT.Square, m)
            m1 = tt(q, r, r, ALU.mult, m)
            ms[c2] = tt(h1[1][:, z], q, h1[0][:, z].bitcast(F32), ALU.subtract, m1, mh)
            return m

        project("mlp_w1", 4096, hh, 8, hm, done, first=32 * layer)
        acc = [bank() for _ in range(4)]
        for s in range(32):
            j, mw = get("mlp_w2", 32 * layer + s, 1024)
            P.join(mw, ms[s // 2], [a[2] for a in acc] if s == 0 else None)
            for c in range(8):
                last = mm3(acc[c // 2][1][:, (c % 2) * 256:(c % 2) * 256 + 256], wsp(j, c * 128, 128), sp(h1, s),
                           s == 0 and c % 2 == 0, s == 31 and c % 2 == 1, mark=c == 7, loose=True)
            put(j, last)
            tick()
        drain2()
        g0 = 48 * layer + 40
        for c in range(8):
            src = acc[c // 2][1][:, (c % 2) * 256:(c % 2) * 256 + 256]
            g = mod[:, g0 + c:g0 + c + 1]
            if unpermute:
                u = sq[:, c * 256:c * 256 + 256]
                m = stt(u, src, g, xs3[:, c, :], ALU.mult, ALU.add, last)
                m = cp(xs3[:, c, :].rearrange("p (l s r) -> p l s r", l=16, s=4),
                       u.rearrange("p (r s l) -> p l s r", r=4, s=4), m)
            else:
                m = stt(xs3[:, c, :], src, g, xs3[:, c, :], ALU.mult, ALU.add, last)
            if c % 2:
                banks.give(acc[c // 2][0], m)
                squares(c // 2, m, rb.rearrange("p b n -> p (b n)"), now=True)

    side2.append(chain(ada(0, 40, 8), ada(1, 0, 16)))
    every[0] = 2
    mlp(0, False)

    phase()
    hh = [carve(2048, F32R), carve(2048, F32R)]
    qk = carve(6 * 2048).rearrange("p (z c t) -> p z c t", z=6, c=8)
    vt = carve(3 * 2048).rearrange("p (g t n) -> p g t n", g=3, t=2)
    B = carve(16 * 512).rearrange("p (h n) -> p h n", h=16)
    step = carve(1024, F32R).rearrange("p (g q) -> p g q", g=8)
    ot = carve(768)
    work = carve(3072)
    m, gn, sf = mod_cols(1, 0, vc("norm_mix", 8, 8))
    m_gq = ts(vc("dil_g_q", 0, 3), vc("dil_g_q", 0, 3), 0.125, None, ALU.mult, None)
    hm = norm_x(gn, sf, hh, m, sq=work[:, 0:2048], tmp=work[:, 2048:2816])
    maskc = carve(512)
    m_mask = [sem_dma(G, gp, "c11", maskc, d["mask"][:, 0:512])]
    dt_ = ot[:, 0:384]
    tabs = [carve(192, F32R), carve(192, F32R)]
    tab = [x.rearrange("p (k e h) -> p k e h", k=4, e=3) for x in tabs]
    mt = sem_dma(G, gp, "c4", dt_, d["tables"])
    m_tab = tt(dt_[:, 0:192], dt_[:, 0:192], dt_[:, 192:384], ALU.subtract, mt)
    m_tabh = act(tabs[0], dt_[:, 0:192], ACT.Copy, m_tab)
    m_tab = tt(tabs[1], dt_[:, 0:192], tabs[0].bitcast(F32), ALU.subtract, m_tabh)
    pI = ot[:, 384:705].bitcast(I32)
    mpi = sem_dma(G, gp, "c5", pI, d["pos_rows"])
    pF = carve(320)
    m1 = ts(pI[:, 320:321], pI[:, 320:321], -1, None, ALU.bitwise_xor, None, mpi)
    m1 = tt(pI[:, 0:320], pI[:, 0:320], pI[:, 320:321].broadcast_to([128, 320]), ALU.add, m1)
    m_pos = cp(pF, pI[:, 0:320], m1)
    bmark = {}

    steps = [step[:, 0:4, :], step[:, 4:8, :]]

    def bias(t):
        if t:
            m_mask.append(sem_dma(G, gp, "c11", maskc, d["mask"][:, 512:1024], bmark[0]))
        used = [P.last, P.last]
        wait = None

        def compare(gq, e):
            g0 = gq * 8 + 4 * e
            pq = pF[:, 64 + t * 128:64 + t * 128 + 128].unsqueeze(1).broadcast_to([128, 4, 128])
            pk = pF[:, g0:g0 + 4].unsqueeze(2).broadcast_to([128, 4, 128])
            return stt(steps[e], pq, cc("lo"), pk, ALU.add, ALU.is_le, m_pos, used[e])

        def evac(gq, b, ps, own, last):
            mk = maskc[:, gq * 32:gq * 32 + 32].unsqueeze(1).broadcast_to([128, 16, 32])
            m = tt(B[:, :, gq * 32:gq * 32 + 32], ps.rearrange("p (c h) -> p h c", h=16), mk, ALU.add, last[0],
                   m_mask, uses)
            banks.give(b, m)
            for half, (b, ps) in enumerate(own):
                for e in range(2):
                    cq = 256 + 128 * e + (gq % 4) * 32 + 16 * half
                    mk = maskc[:, cq:cq + 16].unsqueeze(1).broadcast_to([128, 16, 16])
                    m = tt(B[:, :, cq:cq + 16], ps.rearrange("p (c e h) -> p e h c", e=2, h=16)[:, e, :, :], mk,
                           ALU.add, last[1])
                banks.give(b, m)
            bmark[t] = m

        uses = P.last
        ready_ = [compare(0, 0), compare(0, 1)]
        yield
        for gq in range(8):
            b, ps, fr = bank()
            own = []
            last = [None, None]
            for half in range(2):
                P.join(fr, ready_[half], m_tab)
                for g in range(4):
                    c = (4 * half + g) * 64
                    for e in range(2):
                        last[0] = mm(ps[:, c:c + 64], steps[half][:, g, :], tab[e][:, :, 0, :], e == 0, e == 1,
                                     mark=g == 3 and e == 1)
                if gq // 4 == t:
                    b1, ps1, fr1 = bank()
                    own.append((b1, ps1))
                    P.join(fr1)
                    for g in range(4):
                        for e in range(2):
                            last[1] = mm(ps1[:, g * 128:g * 128 + 128], steps[half][:, g, :], tab[e][:, :, 1:3, :],
                                         e == 0, e == 1, mark=g == 3 and e == 1)
                used[half] = P.last
            if wait:
                evac(*wait)
            wait = (gq, b, ps, own, last)
            if gq < 7:
                ready_ = [compare(gq + 1, 0), compare(gq + 1, 1)]
            yield
        evac(*wait)
        yield

    side.append(bias(0))
    qmarks = {}
    vmarks = []
    qsl = Slots([0, 3])
    qsl.free[0][1].append(m_pos)
    qsl.free[1][1].append(m_pos)
    wk = [work[:, i * 512:(i + 1) * 512] for i in range(6)]

    def qk_done(zi):
        got = []

        def done(c2, ps, last):
            n, qf = qsl.take()
            m = act(wk[n], ps, ACT.Square, last, qf)
            got.append((n, c2, ps))
            return m

        def own(m, b):
            n, c2, ps = got.pop()
            pend.append([0, lambda: finish(m, b, n, c2, ps)])

        def finish(m, b, n, c2, ps):
            gc = vc("dil_g_q" if zi % 2 == 0 else "dil_g_k", zi // 2)
            b2, ps2, fr2 = bank()
            m2 = mm(ps2, blk, wk[n], True, True, m, fr2, mark=True)
            m3 = act(wk[n + 1], ps2, ACT.Identity, m2, scale=1.0 / 64, bias=eps)
            banks.give(b2, m3)
            m4 = act(wk[n + 2], wk[n + 1], ACT.Abs_reciprocal_sqrt, m3)
            m5 = act(wk[n], wk[n + 2], ACT.Square, m4)
            m5 = stt(wk[n], wk[n + 1], -0.5, wk[n], ALU.mult, ALU.mult, m5)
            m5 = stt(wk[n], wk[n], 1.5, wk[n + 2], ALU.add, ALU.mult, m5)
            m5 = stt(qk[:, zi, 2 * c2:2 * c2 + 2, :].rearrange("p c t -> p (c t)"), ps, gc, wk[n], ALU.mult,
                     ALU.mult, m5)
            qmarks[zi] = m5
            qsl.give(n, m5)
            banks.give(b, m5)

        return done, [own]

    side2.append(ada(1, 16, 16))
    every[0] = 4
    for g in range(3):
        for z in range(2):
            done, own = qk_done(2 * g + z)
            project("dil_qk", 1024, hh, 8, hm, done, first=8 * (2 * g + z), own=own)
        vmarks += project_tok("dil_v", 1024, hh, hm, vt[:, g].rearrange("p t n -> p (t n)"), first=8 * g)
    flush()
    drain_side()
    side2.append(ada(1, 32, 8))
    every[0] = 3

    st = carve(64).rearrange("p (t s h) -> p t s h", t=2, s=2)
    NB = 3
    sbuf, ptb = wk[0:3], wk[3:6]
    sfree, pfree = Slots(range(NB)), Slots(range(NB))
    hold, acc = {}, {}
    outs = []

    def s1(u):
        t, h = divmod(u, 16)
        tile = slice(t * 128, t * 128 + 128)
        b, ps, fr = bank()
        r0 = (h % 2) * 64
        P.join(fr, [qmarks[z] for z in range(6)])
        for g in range(3):
            q = qk[r0:r0 + 64, 2 * g, h // 2, tile]
            k = qk[r0:r0 + 64, 2 * g + 1, h // 2, slice(0, 256) if g == 0 else tile]
            o = ps[:, 0:256] if g == 0 else ps[:, 128 + g * 128:256 + g * 128]
            last = mm(o, q, k, True, True, mark=g == 2)
        i, sf = sfree.take()
        m = ttr(sbuf[i], ps, B[:, h, :], ALU.add, ALU.max, -3e38, st[:, t, 0, h:h + 1], last, sf, bmark[t])
        banks.give(b, m)
        m = ts(st[:, t, 0, h:h + 1], st[:, t, 0, h:h + 1], -1.0, None, ALU.mult, None, m)
        m = act(sbuf[i], sbuf[i], ACT.Exp, m, bias=st[:, t, 0, h:h + 1], accum_out=st[:, t, 1, h:h + 1])
        hold[u] = (i, m)

    def s2(u):
        i, m = hold[u]
        b, ps, fr = bank()
        P.join(fr, m)
        for kb in range(4):
            last = tr(ps[:, kb * 128:kb * 128 + 128], sbuf[i][:, kb * 128:kb * 128 + 128], mark=kb == 3)
        sfree.give(i, last)
        j, pf = pfree.take()
        m = act(ptb[j], ps, ACT.Copy, last, pf)
        banks.give(b, m)
        hold[u] = (j, m)

    def s1b(u):
        t, h = divmod(u, 16)
        i, m = hold[u]
        m = recip(st[:, t, 1, h:h + 1], st[:, t, 1, h:h + 1], m)
        hold[u] = (i, ts(sbuf[i], sbuf[i], st[:, t, 1, h:h + 1], None, ALU.mult, None, m))

    def s3(u):
        t, h = divmod(u, 16)
        j, m = hold.pop(u)
        if h % 8 == 0:
            acc[0] = bank()
        b, ps, fr = acc[0]
        P.join(m, fr, vmarks)
        r, c = (h % 2) * 64, (h % 8) // 2
        for kb in range(4):
            v = vt[:, 0, kb, h * 64:h * 64 + 64] if kb < 2 else vt[:, kb - 1, t, h * 64:h * 64 + 64]
            last = mm(ps[r:r + 64, c * 128:c * 128 + 128], v, ptb[j][:, kb * 128:kb * 128 + 128], kb == 0, kb == 3,
                      mark=kb == 3)
        pfree.give(j, last)
        if h % 8 == 7:
            c0 = h // 8 * 4
            v3 = [x.rearrange("p (c t) -> p c t", c=8)[:, c0:c0 + 4, t * 128:t * 128 + 128] for x in hh]
            p3 = ps.rearrange("p (c t) -> p c t", c=4)
            m = act(v3[0], p3, ACT.Copy, last)
            m = tt(v3[1], p3, v3[0].bitcast(F32), ALU.subtract, m)
            banks.give(b, m)
            outs.append(m)

    for n in range(35):
        if n == 16:
            side.append(bias(1))
            drain_side()
        if n < 32:
            s1(n)
        if 0 <= n - 1 < 32:
            s1b(n - 1)
        if 0 <= n - 2 < 32:
            s2(n - 2)
        if 0 <= n - 3 < 32:
            s3(n - 3)
        tick()
    drain2()
    project("dil_w_o", 1024, hh, 8, [outs] * 8, residual(lambda c: mod[:, 64 + c:65 + c], work))
    side2.append(ada(1, 40, 8))
    every[0] = 4
    mlp(1, True)
    every[0] = 1

    phase()
    memT = [carve(2048, F32R), carve(2048, F32R)]
    memx = carve(2048)
    mt_ = memx.rearrange("p (t n) -> p t n", t=2)
    m_mem = sem_dma(G, gp, "c8", mt_, d["mem"])
    keep, scope[0] = scope[0], ExitStack()
    sq = carve(2048)
    hh = [carve(2048, F32R), carve(2048, F32R)]
    hm = norm_x(lambda k: vc("norm_mix_2", k), None, hh, sq=sq, tmp=carve(768))
    gw = carve(1024).rearrange("p (z n) -> p z n", z=8)
    m_gw = sem_dma(G, gp, "c6", gw.rearrange("p z n -> p (z n)"), d["gates"])
    B2 = carve(8 * 512).rearrange("p (h t n) -> p h t n", h=8, t=2)
    mB = sem_dma(G, gp, "c7", B2.rearrange("p h t n -> p (h t n)"), d["rb"])

    xp = carve(4 * 260).rearrange("p (c t) -> p c t", c=4)
    m = fill(xp[:, :, 0:3], 0.0)
    ge = carve(1024).rearrange("p (c t) -> p c t", c=4)
    q2 = carve(1024).rearrange("p (c t) -> p c t", c=4)
    k2 = carve(1024).rearrange("p (c t) -> p c t", c=4)
    v2 = carve(1024).rearrange("p (t n) -> p t n", t=2)
    marks = {"x": [], "g": [], "q": [], "k": []}

    def done(c2, ps, last):
        kind = "xgqk"[c2 // 2]
        c = 2 * (c2 % 2)
        p3 = ps.rearrange("p (c t) -> p c t", c=2)
        if kind == "x":
            m = act(xp[:, c:c + 2, 3:259], p3, ACT.Copy, last)
        elif kind == "g":
            m = act(ge[:, c:c + 2, :], p3, ACT.Gelu_apprx_tanh, last)
        else:
            dst = q2 if kind == "q" else k2
            m = act(dst[:, c:c + 2, :], p3, ACT.Copy, last, scale=0.125 if kind == "q" else 1.0)
        marks[kind].append(m)
        return m

    lt = carve(4 * 8).rearrange("p (z n) -> p z n", z=8)
    xc = carve(1024).rearrange("p (c t) -> p c t", c=4)
    ra = carve(1024).rearrange("p (c t) -> p c t", c=4)
    ia = carve(1024).rearrange("p (c t) -> p c t", c=4)
    La = carve(1024).rearrange("p (c t) -> p c t", c=4)
    fl = lambda z: z.rearrange("p c t -> p (c t)")
    lru_m = []

    def lru():
        lam = vc("lam", 0, 4)
        m = ts(lt[:, 0], lam, -1.0, 0.0, ALU.mult, ALU.max)
        m = act(lt[:, 1], lam, ACT.Abs)
        m = act(lt[:, 1], lt[:, 1], ACT.Exp, m, scale=-1.0)
        m = ts(lt[:, 2], lt[:, 1], 2.0, None, ALU.add, None, m)
        m = recip(lt[:, 3], lt[:, 2], m)
        m = tt(lt[:, 3], lt[:, 3], lt[:, 1], ALU.mult, m)
        m = tt(lt[:, 4], lt[:, 3], lt[:, 3], ALU.mult, m)
        m = ts(lt[:, 5], lt[:, 4], 1.0 / 15, 1.0 / 13, ALU.mult, ALU.add, m)
        for n in (11, 9, 7, 5, 3, 1):
            m = tt(lt[:, 5], lt[:, 5], lt[:, 4], ALU.mult, m)
            m = ts(lt[:, 5], lt[:, 5], 1.0 / n, None, ALU.add, None, m)
        m = tt(lt[:, 5], lt[:, 5], lt[:, 3], ALU.mult, m)
        m = stt(lt[:, 6], lt[:, 5], 2.0, lt[:, 0], ALU.mult, ALU.add, m)
        m_sp = ts(lt[:, 7], lt[:, 6], 8.0, None, ALU.mult, None, m)

        yield
        for c in range(4):
            if c:
                yield
            m = ts(xc[:, c, :], xp[:, c, 0:256], vc("conv_w", c), vc("conv_b", c), ALU.mult, ALU.add, marks["x"])
            for j in range(1, 4):
                m = stt(xc[:, c, :], xp[:, c, j:j + 256], vc("conv_w", 4 * j + c), xc[:, c, :], ALU.mult, ALU.add, m)
            yield
            b, ps, fr = bank()
            P.join(fr, m, m_gw)
            mm(ps[:, 0:256], gw[:, c, :], xc[:, c, :], True, True)
            last = mm(ps[:, 256:512], gw[:, 4 + c, :], xc[:, c, :], True, True, mark=True)
            act(ra[:, c, :], ps[:, 0:256], ACT.Sigmoid, last, bias=vc("gate_a_b", c))
            m = act(ia[:, c, :], ps[:, 256:512], ACT.Sigmoid, bias=vc("gate_x_b", c))
            banks.give(b, m)
            m_l = ts(La[:, c, :], ra[:, c, :], lt[:, 7, c:c + 1], None, ALU.mult, None, m, m_sp)
        yield
        m_a = act(fl(ra), fl(La), ACT.Exp, m_l, scale=-1.0)
        m_t = act(fl(La), fl(La), ACT.Tanh, m_a)
        m = tt(fl(ia), fl(ia), fl(xc), ALU.mult, m_t)
        m = tt(fl(xc), fl(ra), fl(ra), ALU.mult, m)
        yield
        m = stt(fl(xc), fl(xc), 1.0, fl(La), ALU.add, ALU.mult, m)
        m = act(fl(xc), fl(xc), ACT.Sqrt, m)
        yield
        m = tt(fl(ia), fl(ia), fl(xc), ALU.mult, m)
        for c in range(4):
            m2 = scan(La[:, c, :], ra[:, c, :], ia[:, c, :], m)
        m = tt(fl(La), fl(La), fl(ge), ALU.mult, m2, marks["g"])
        lru_m.append(m)
        yield

    mm_ = []

    def memory():
        for t in range(2):
            m = act(fl(ia), mt_[:, t, :], ACT.Square, m_mem, A.last, scale=1.0 / 32, accum_out=sm[:, t:t + 1])
        _, m = rsqrt(sm[:, 2:4], sm[:, 0:2], 1.0, sm[:, 4:6], sm[:, 6:8], m)
        yield
        for t in range(2):
            m2 = ts(mt_[:, t, :], mt_[:, t, :], sm[:, 2 + t:3 + t], None, ALU.mult, None, m)
        yield
        for c in range(0, 8, 2):
            mm_.extend(to_feature(mt_[:, :, c * 128:], 2, 128, [z[:, c * 256:c * 256 + 512] for z in memT], m2,
                                  gain=lambda k, c=c: vc("memn", c + k), split=True))
            yield

    sm = carve(8)
    side2.append(memory())
    project("w_in_2", 512, hh, 8, hm, done)
    fill(B2[:, :, 0, 128:256], NEG, mB)
    fill(B2[0:64, :, 0, 64:128], NEG)
    m_B2 = fill(B2[0:64, :, 1, 192:256], NEG)
    while side2:
        tick2()
    side.append(lru())

    def later(off):
        return lambda c2, ps, last: done(c2 + off, ps, last)

    project("w_in_2", 1536, hh, 8, hm, later(2), first=4)
    m_v2 = project_tok("w_in_2v", 512, hh, hm, v2.rearrange("p t n -> p (t n)"))

    def chunk_scores(h, ps):
        r0 = (h % 2) * 64
        for t in range(2):
            m = mm(ps[:, t * 256:t * 256 + 256], q2[r0:r0 + 64, h // 2, t * 128:t * 128 + 128],
                   k2[r0:r0 + 64, h // 2, :], True, True, mark=t == 1)
        return m

    def attended(c2, ps, last):
        return act(at_[:, c2 * 512:c2 * 512 + 512], ps, ACT.Copy, last)

    at_ = carve(1024)
    om = attention(8, chunk_scores, B2, 1.0, lambda h, kb: v2[:, kb, h * 64:h * 64 + 64], 64, attended,
                   [marks["q"], marks["k"], m_v2, m_B2])
    drain_side()
    y = [carve(2048, F32R), carve(2048, F32R)]
    ya = norm(fl(La), 4, lambda k: vc("grp_a", k), None, [z[:, 0:1024] for z in y], lru_m, sq=fl(xc), tmp=sq[:, 0:768])
    yb = norm(at_, 4, lambda k: vc("grp_b", k), None, [z[:, 1024:2048] for z in y], om, sq=fl(ra), tmp=sq[:, 768:1536])
    ev = {"k": [], "q": []}

    def evac(dst, key):
        def done(c2, ps, last):
            m = act(dst[:, 2 * c2:2 * c2 + 2, :], ps.rearrange("p (c t) -> p c t", c=2), ACT.Copy, last)
            ev[key].append(m)
            return m
        return done

    kM = memx.rearrange("p (k t) -> p k t", k=8)
    project("w_mem_k", 1024, memT, 8, mm_, evac(kM, "k"))
    project("w_out_2", 1024, y, 8, ya + yb, residual(None, fl(xc)))

    phase()
    hh = [carve(2048, F32R), carve(2048, F32R)]
    hm = norm_x(lambda k: vc("cross", k), None, hh, sq=carve(2048), tmp=carve(768))
    sq = carve(1024)
    qM = carve(2048).rearrange("p (k t) -> p k t", k=8)
    vM = carve(2048).rearrange("p (t n) -> p t n", t=2)
    m_vM = project_tok("w_mem_v", 1024, memT, mm_, vM.rearrange("p t n -> p (t n)"))
    project("w_q_mem_2", 1024, hh, 8, hm, evac(qM, "q"))
    def mem_scores(h, ps):
        for t in range(2):
            for k in range(2):
                m = mm(ps[:, t * 256:t * 256 + 256], qM[:, 2 * h + k, t * 128:t * 128 + 128], kM[:, 2 * h + k, :],
                       k == 0, k == 1, mark=t == 1 and k == 1)
        return m

    om = attention(4, mem_scores, None, 1.0 / 16, lambda h, kb: vM[:, kb, h * 256:h * 256 + 256], 256, split_out(memT),
                   [ev["q"], ev["k"], m_vM])
    project("w_o_mem_2", 1024, memT, 8, om, residual(None, sq))

    phase(keep, lent)
    C = carve(128 * 256)
    C3 = C.rearrange("p (i t) -> p i t", i=128)
    tail = [C[:, (64 + 8 * z) * 256:] for z in range(8)]
    sq, skT, qP, sc = tail[0][:, 0:2048], tail[1][:, 0:2048], tail[2][:, 0:4096], tail[6][:, 0:4096]
    tmp = tail[4][:, 0:768]
    skT = skT.rearrange("p (z n) -> p z n", z=16)
    qP = qP.rearrange("p (z t) -> p z t", z=16)
    sc = sc.rearrange("p (t z n) -> p t z n", t=2, z=16)
    m_sk = sem_dma(G, gp, "c9", skT.rearrange("p z n -> p (z n)"), d["skT"])
    sel = carve(768).rearrange("p (s t n) -> p s t n", s=3, t=2)
    selT = carve(768).rearrange("p (s t) -> p s t", s=3)
    mr, cand = carve(256), carve(256)
    eq = carve(256).rearrange("p (a b) -> p a b", a=16)
    tv = carve(32).rearrange("p (s n) -> p s n", s=2)
    ti = carve(32, U32).rearrange("p (s n) -> p s n", s=2)
    tif = carve(32).rearrange("p (s n) -> p s n", s=2)
    pp = carve(3 * 16, U32).rearrange("p (s n) -> p s n", s=3)
    pf_ = carve(32).rearrange("p (s n) -> p s n", s=2)
    gs = carve(32)
    fs = carve(8)
    iota = cc("iota", 0, 16)
    keep, scope[0] = scope[0], ExitStack()
    hh = [carve(2048, F32R), carve(2048, F32R)]
    hm = norm_x(lambda k: vc("ffn", k), None, hh, sq=sq, tmp=tmp)
    ev["p"] = []
    project("w_query_2", 2048, hh, 8, hm, evac(qP, "p"))
    sc_m = {}
    for t in range(2):
        for z4 in range(4):
            b, ps, fr = bank()
            P.join(fr, m_sk, ev["p"])
            for z in range(4):
                last = mm(ps[:, z * 128:z * 128 + 128], qP[:, 4 * z4 + z, t * 128:t * 128 + 128], skT[:, 4 * z4 + z, :],
                          True, True, mark=z == 3)
            m = act(sc[:, t, 4 * z4:4 * z4 + 4, :], ps.rearrange("p (z n) -> p z n", z=4), ACT.Copy, last)
            banks.give(b, m)
            sc_m[t, z4] = m

    def vmax(o, a, *waits):
        return V(lambda: ve.max(o, a), *waits)

    def vidx(o, mx, a, *waits):
        return V(lambda: ve.max_index(o, mx, a), *waits)

    def vrep(o, mx, a, *waits):
        return V(lambda: ve.match_replace(o, mx, a, -3e38), *waits)

    def top16(n, src, dstv, dsti, *waits):
        m = vmax(dstv[:, 0:8], src, waits)
        m1 = vidx(dsti[:, 0:8], dstv[:, 0:8], src, m)
        m2 = vrep(mr[:, 0:n], dstv[:, 0:8], src, m1)
        yield
        m3 = vmax(dstv[:, 8:16], mr[:, 0:n], m2)
        vidx(dsti[:, 8:16], dstv[:, 8:16], mr[:, 0:n], m3)
        yield

    def topk():
        for n in range(16):
            t, h = divmod(n, 8)
            for z in range(2):
                yield from top16(128, sc[:, t, 2 * h + z, :], tv[:, z, :], ti[:, z, :], V.last, sc_m[t, h // 2])
            m = cp(tif, ti, V.last)
            m1 = tt(cand.rearrange("p (a b) -> p a b", a=16), tv[:, 0, :].unsqueeze(2).broadcast_to([128, 16, 16]),
                    tv[:, 1, :].unsqueeze(1).broadcast_to([128, 16, 16]), ALU.add, m)
            yield
            tp = sel[:, 2, t, h * 16:h * 16 + 16]
            yield from top16(256, cand, tp, pp[:, 0, :], m1)
            m = ts(pp[:, 1, :], pp[:, 0, :], 4, None, ALU.logical_shift_right, None, V.last)
            m = ts(pp[:, 2, :], pp[:, 0, :], 15, None, ALU.bitwise_and, None, m)
            m = cp(pf_, pp[:, 1:3, :], m)
            for z in range(2):
                yield
                m = tt(eq, pf_[:, z, :].unsqueeze(2).broadcast_to([128, 16, 16]),
                       iota.unsqueeze(1).broadcast_to([128, 16, 16]), ALU.is_equal, m)
                m = tt(eq, eq, tif[:, z, :].unsqueeze(1).broadcast_to([128, 16, 16]), ALU.mult, m)
                m = red(sel[:, z, t, h * 16:h * 16 + 16], eq, ALU.add, m)
            yield

    side.append(topk())

    def gelu(c2, ps, last):
        tick()
        if c2 == 55:
            drain_side()
        m = act(C[:, c2 * 512:c2 * 512 + 512], ps, ACT.Gelu_apprx_tanh, last, sc_m[1, 3], V.last if c2 >= 30 else None)
        gm.append(m)
        return m

    gm = []
    project("eu", 16384, hh, 8, hm, gelu)
    drain_side()

    g4 = sel[:, 2, :, :].rearrange("p t (h n) -> p (t h) n", h=8)
    gd = mr.rearrange("p (h n) -> p h n", n=16)
    m = tt(gd, g4, g4[:, :, 0:1].broadcast_to([128, 16, 16]), ALU.subtract, V.last)
    m = act(gd, gd, ACT.Exp, m)
    m = red(gs[:, 0:16], gd, ALU.add, m)
    m = recip(gs[:, 16:32], gs[:, 0:16], m)
    m = tt(g4, gd, gs[:, 16:32].unsqueeze(2).broadcast_to([128, 16, 16]), ALU.mult, m)
    msel = []
    for s, n in ((0, 2), (2, 1)):
        b, ps, fr = bank()
        P.join(fr, m)
        for z in range(n):
            for t in range(2):
                last = tr(ps[:, z * 256 + t * 128:z * 256 + t * 128 + 128], sel[:, s + z, t, :],
                          mark=z == n - 1 and t == 1)
        mk = cp(selT[:, s:s + n, :], ps[:, 0:n * 256].rearrange("p (s t) -> p s t", s=n), last)
        banks.give(b, mk)
        msel.append(mk)

    def times(b, ps, last, v, q):
        m = tt(v, ps.rearrange("p (t i) -> p t i", t=4), v, ALU.mult, last, gm if q == 0 else None)
        banks.give(b, m)
        return m

    scope[0].close()
    scope[0] = ExitStack()
    one = [carve(1024).rearrange("p (s t n) -> p s t n", s=2, t=4) for _ in range(4)]
    dist = [carve(128) for _ in range(2)]
    minus = cand[:, 0:256], eq.rearrange("p a b -> p (a b)")
    G.join(P.last, A.last, V.last)
    A.join(P.last, V.last)
    V.join(P.last)
    m_neg = [ts(minus[z], selT[:, 2 * z, :], -1.0, None, ALU.mult, None, msel) for z in range(2)]
    of = Slots(range(4))
    Ct = C.rearrange("p (i t) -> p t i", i=128)
    for q in range(64):
        b, ps, fr = bank()
        k, ofr = of.take()
        o1, o2 = one[k][:, 0], one[k][:, 1]
        ms = [tt(o2[:, 0:3], cc("iota").unsqueeze(1).broadcast_to([128, 3, 128]),
                 selT[:, 1, 4 * q:4 * q + 3].unsqueeze(2).broadcast_to([128, 3, 128]), ALU.is_equal, ofr, msel),
              gts(o2[:, 3], cc("iota"), selT[:, 1, 4 * q + 3:4 * q + 4], None, ALU.is_equal, None, ofr, msel)]
        for i in range(4):
            t = 4 * q + i
            if i == 1 or (i == 3 and q % 4):
                dist.append(dist.pop(0))
                m = act(dist[0], cc("iota"), ACT.Abs, m_neg, bias=minus[0][:, t:t + 1])
                m = act(o1[:, i, :], dist[0], ACT.Relu, m, ofr, scale=minus[1][:, t:t + 1],
                        bias=selT[:, 2, t:t + 1])
            elif i != 2:
                m = ts(o1[:, i, :], cc("iota"), selT[:, 0, t:t + 1], selT[:, 2, t:t + 1], ALU.is_equal, ALU.mult,
                       ofr, msel)
            else:
                m = gts(o1[:, i, :], cc("iota"), selT[:, 0, t:t + 1], selT[:, 2, t:t + 1], ALU.is_equal, ALU.mult,
                        ofr, msel)
            ms.append(m)
        P.join(fr, ms)
        for i in range(4):
            last = mm(ps[:, i * 128:i * 128 + 128], o2[:, i, :], o1[:, i, :], True, True, mark=i == 3)
        of.give(k, last)
        if q:
            mc = times(*held)
        held = (b, ps, last, Ct[:, 4 * q:4 * q + 4, :], q)
    mc = times(*held)

    scope[0].close()
    scope[0] = ExitStack()
    NC = 4
    cs = [[carve(256, F32R), carve(256, F32R)] for _ in range(NC)]
    nf = carve(1024)
    G.join(mc)
    m_nf = sem_dma(G, gp, "c10", nf, d["norm_final"])
    acc = [[bank(), bank()] for _ in range(2)]
    for t in range(2):
        for e in range(2):
            P.join(acc[t][e][2])
            for c in range(4):
                k = 4 * e + c
                mm(acc[t][e][1][:, c * 128:c * 128 + 128], xs3[:, k, t * 128:t * 128 + 128], ident, c == 0, False,
                   loose=True)
    cfree = Slots(range(NC))
    cm = {}

    def coef(i):
        k, fr = cfree.take()
        x = C3[:, i, :]
        m = act(cs[k][0], x, ACT.Copy, mc, fr)
        m = tt(cs[k][1], x, cs[k][0].bitcast(F32), ALU.subtract, m, fr)
        cm[i] = (k, m)

    for i in range(2):
        coef(i)
    for i in range(128):
        if i + 2 < 128:
            coef(i + 2)
        j, mw = get("ev", i, 1024)
        k, m = cm.pop(i)
        P.join(mw, m)
        for t in range(2):
            for e in range(2):
                last = mm3(acc[t][e][1], sp(cs[k], 0, 256, t * 128, 128), wsp(j, e * 512, 512), False, i == 127,
                           mark=t == 1 and e == 1, loose=True)
        put(j, last)
        cfree.give(k, last)
    xt = C[:, 0:2048].rearrange("p (t n) -> p t n", t=2)
    for t in range(2):
        for e in range(2):
            m = act(C[:, 2048:2560], acc[t][e][1], ACT.Square, last, A.last, scale=1.0 / 32,
                    accum_out=fs[:, 2 * t + e:2 * t + e + 1])
    m = tt(fs[:, 4:6], fs[:, 0:4:2], fs[:, 1:4:2], ALU.add, m)
    m = act(gs[:, 0:2], fs[:, 4:6], ACT.Sqrt, m, bias=eps)
    m = recip(gs[:, 2:4], gs[:, 0:2], m)
    for t in range(2):
        for e in range(2):
            z = slice(e * 512, e * 512 + 512)
            m1 = stt(xt[:, t, z], acc[t][e][1], gs[:, 2 + t:3 + t], nf[:, z], ALU.mult, ALU.mult, m, m_nf)
        sem_dma(S, sy, "out", out[0, t * 128:t * 128 + 128, :], xt[:, t, :], m1)
    S.join(("out", 32))
    scope[0].close()
    keep.close()
    if dry:
        ctx.close()
        return

    assert at["get"] == len(plan)
    names = ["V", "A", "P", "G"] + sorted(sem_uses)
    sems = {n: ctx.enter_context(nc.semaphore("s_" + n)) for n in names}
    blockc = ctx.enter_context(nc.Block())

    def emit(q, eng):
        known = {}
        for fn, waits, inc in q.items:
            for sname, v in waits:
                if v > known.get(sname, 0):
                    eng.wait_ge(sems[sname], v)
                    known[sname] = v
            if fn is None:
                continue
            ins = fn()
            if inc is not None:
                ins.then_inc(sems[inc[0]], inc[1])

    @blockc.sync
    def _(e):
        emit(S, e)

    @blockc.scalar
    def _(e):
        emit(A, e)

    @blockc.vector
    def _(e):
        emit(V, e)

    @blockc.gpsimd
    def _(e):
        emit(G, e)

    @blockc.tensor
    def _(e):
        emit(P, e)

    ctx.close()


TOK = np.array([r + 4 * s + 16 * l for r in range(4) for s in range(4) for l in range(16)])


def constants():
    con = np.zeros((128, NCON), np.float32)

    def put(name, a):
        at, n = CON[name]
        con[:, at:at + n] = np.asarray(a, np.float32).reshape(128, n)

    p = np.arange(128)
    put("ident", np.eye(128))
    put("ones", np.ones((128, 128)))
    put("blk", p[:, None] // 64 == p[None, :] // 64)
    half = np.arange(16, dtype=np.float32) / np.float32(16)
    put("invf", np.broadcast_to(np.float32(1) / (np.float32(10000.0) ** half), (128, 16)))
    seq, lows = bucket_order()
    low = np.full(32, 1e30)
    low[0] = -1e30
    low[1:31] = lows[1:]
    put("lo", np.tile(low, 4)[:, None])
    put("eps", np.full((128, 1), 1e-6))
    put("iota", np.broadcast_to(np.arange(128), (128, 128)))
    return con


def window_mask():
    q = TOK.reshape(2, 128)
    mask = np.zeros((2, 128, 512))
    for t in range(2):
        mask[t, :, 0:256] = np.where(np.abs(q[t][:, None] - TOK[None, :]) <= 64, 0, NEG)
        mask[t, :, 256:384] = np.where(q[t][:, None] % 4 == q[t][None, :] % 4, 0, NEG)
        mask[t, :, 384:512] = np.where(q[t][:, None] % 16 == q[t][None, :] % 16, 0, NEG)
    return np.ascontiguousarray(mask.transpose(1, 0, 2).reshape(128, 1024).astype(np.float32))


def bucket_order():
    first = list(range(8)) + [15, 27, 50, 91, 166, 305, 559]
    first = list(range(9)) + [15, 27, 50, 91, 166, 305, 559]
    seq, lows = [], []
    for b in range(15, -1, -1):
        seq.append(b)
        lows.append(-(first[b + 1] - 1) if b < 15 else -(1 << 30))
    for b in range(1, 16):
        seq.append(16 + b)
        lows.append(first[b])
    return seq, lows


def stationary(w, cols=128):
    k, n = w.shape
    return np.ascontiguousarray(w.reshape(k // 128, 128, n // cols, cols).transpose(2, 1, 0, 3)).reshape(
        n // cols, 128, -1)


def moving(w):
    n = w.shape[1]
    return np.ascontiguousarray(w.reshape(2, 4, 128, n // 256, 256).transpose(3, 0, 2, 1, 4)).reshape(-1, 128, 1024)


def lay_out(i):
    i = {k: np.asarray(v) for k, v in i.items()}
    a = {}
    a["ada_w"] = np.ascontiguousarray(i["ada_w"].transpose(0, 2, 1)).reshape(96, 128, 1024)
    a["c_row"] = np.ascontiguousarray(i["c"])
    a["mlp_w1"] = np.concatenate([stationary(w) for w in i["mlp_w1"]])
    a["mlp_w2"] = np.ascontiguousarray(i["mlp_w2"]).reshape(64, 128, 1024)
    w = i["mla_w_in"][0]
    last = np.zeros((1024, 256), np.float32)
    last[:, 0:160] = w[:, 512:672]
    w = moving(np.concatenate([w[:, 0:512], last], 1))
    w[4:6, :, 0:640] = w[4:6].reshape(2, 128, 4, 256)[:, :, :, 0:160].reshape(2, 128, 640)
    a["mla_w_in"] = w
    a["mla_w_qb"] = stationary(i["mla_w_qb"][0], 256)
    a["mla_w_kvb"] = stationary(i["mla_w_kvb"][0], 512)
    a["mla_w_o"] = stationary(i["mla_w_o"][0])
    w = i["dil_w_in"][0].reshape(1024, 3, 3, 1024)
    a["dil_qk"] = stationary(w[:, :, 0:2, :].reshape(1024, 6144))
    a["dil_v"] = moving(w[:, :, 2, :].reshape(1024, 3072))
    a["dil_w_o"] = stationary(i["dil_w_o"][0])
    a["w_in_2"] = stationary(i["w_in_2"][0][:, 0:2048])
    a["w_in_2v"] = moving(i["w_in_2"][0][:, 2048:2560])
    a["w_out_2"] = stationary(i["w_out_2"][0])
    a["w_mem_k"] = stationary(i["w_kv_mem_2"][0][:, 0:1024])
    a["w_mem_v"] = moving(i["w_kv_mem_2"][0][:, 1024:2048])
    for n in ("w_q_mem_2", "w_o_mem_2", "w_query_2"):
        a[n] = stationary(i[n][0])
    a["eu"] = np.ascontiguousarray(i["expert_u_2"][0].reshape(128, 128, 8, 128).transpose(0, 3, 2, 1)).reshape(
        128, 128, 1024)
    a["ev"] = np.ascontiguousarray(i["expert_v_2"][0].reshape(128, 128, 1024))
    a["mask"] = window_mask()

    def cols(v):
        return np.ascontiguousarray(np.asarray(v).reshape(-1, 128).T)

    vec = np.zeros((128, NVEC), np.float32)

    def put(name, c):
        at, n = VEC[name]
        vec[:c.shape[0], at:at + n] = c

    for name, src in [("norm_mix", "norm_mix"), ("norm_mlp", "norm_mlp"), ("ada_b", "ada_b"),
                      ("g_qa", "mla_g_qa"), ("g_kva", "mla_g_kva"), ("norm_mix_2", "norm_mix_2"),
                      ("conv_w", "conv_w_2"), ("conv_b", "conv_b_2"), ("gate_a_b", "gate_a_b_2"),
                      ("gate_x_b", "gate_x_b_2"), ("lam", "lru_lambda_2"), ("grp_a", "norm_grp_a_2"),
                      ("grp_b", "norm_grp_b_2"), ("cross", "norm_cross_2"), ("memn", "norm_mem_2"),
                      ("ffn", "norm_ffn_2")]:
        put(name, cols(i[src]))
    put("g_q", i["mla_g_q"].T)
    put("g_k", i["mla_g_k"].T)
    put("dil_g_q", np.concatenate([i["dil_g_q"][0].T] * 2, 0))
    put("dil_g_k", np.concatenate([i["dil_g_k"][0].T] * 2, 0))
    a["vec"] = vec
    a["con"] = constants()
    xp = i["x"][0][TOK]
    a["xT"] = np.ascontiguousarray(xp.T.reshape(8, 128, 256).transpose(1, 0, 2).reshape(128, 2048))
    pos = i["positions"][0][TOK].astype(np.int32)
    a["pos_col"] = np.ascontiguousarray(pos.reshape(2, 128).T)
    rows = np.zeros((128, 321), np.int32)
    rows[:, 0:64] = np.repeat(pos.reshape(64, 4).T, 32, axis=0)
    rows[:, 64:320] = pos[None, :]
    rows[:, 320] = pos[0]
    a["pos_rows"] = rows
    seq, _ = bucket_order()
    rb = i["rel_bias"]
    tabs = np.zeros((128, 2, 4, 48), np.float32)
    for k in range(4):
        tabs[32 * k:32 * k + 31, 0, k, :] = rb[seq]
        tabs[32 * k + 1:32 * k + 31, 1, k, :] = rb[seq[:-1]]
    a["tables"] = tabs.reshape(128, 384)
    gates = np.zeros((128, 8, 128), np.float32)
    for z, n in enumerate(("gate_a_w_2", "gate_x_w_2")):
        for b in range(8):
            e = 64 * (b % 2)
            gates[e:e + 64, 4 * z + b // 2, e:e + 64] = i[n][0, b]
    a["gates"] = gates.reshape(128, 1024)
    rel = np.arange(256)[:, None] - np.arange(256)[None, :]
    rb2 = i["rel_bias_2"][0][:, np.clip(rel, -128, 128) + 128].reshape(8, 2, 128, 256)
    a["rb"] = np.ascontiguousarray(rb2.transpose(2, 0, 1, 3).reshape(128, 4096))
    a["mem_2"] = np.ascontiguousarray(i["mem_2"])
    a["skT"] = np.ascontiguousarray(i["sub_keys_2"][0].transpose(3, 0, 1, 2).reshape(128, 2048))
    a["norm_final_2"] = np.ascontiguousarray(i["norm_final_2"])
    return a


def views(t):
    d = dict(t)
    d["mem"] = t["mem_2"].rearrange("b (t p) n -> p (b t) n", p=128)
    d["c_row"] = t["c_row"].broadcast_to([128, 1024])
    d["norm_final"] = t["norm_final_2"].rearrange("(a n) -> a n", a=1).broadcast_to([128, 1024])
    return d


def kernel(**inputs):
    import concourse.bacc as bacc
    from concourse.bass_utils import run_bass_kernel_spmd

    nc = bacc.Bacc("TRN2", target_bir_lowering=False, num_devices=1)
    arrays = {f"in_{n}": v for n, v in lay_out(inputs).items()}
    t = {n[3:]: nc.dram_tensor(n, v.shape, mybir.dt.from_np(v.dtype), kind="ExternalInput").ap()
         for n, v in arrays.items()}
    out = nc.dram_tensor("out_0", (1, 256, 1024), F32, kind="ExternalOutput").ap()
    program(nc, views(t), out)
    r = run_bass_kernel_spmd(nc, [arrays], core_ids=[0])
    return r.results[0]["out_0"]
```
